# Optimizing a Trainium2 kernel written in Bass

```python
import math
import jax, jax.numpy as jnp
from jax import lax
import numpy as np

'''Hybrid streaming-encoder residual block (DEPTH layers, all positions at once).

Per layer:
  h = RMSNorm(x)
  [q,k,v | B,C,u | gate_a,gate_b] = h @ W_in                (one combined input projection)
  branch A: stick-breaking attention, 8 heads x 64, strictly causal, no positional encoding
  branch B: gated short conv  B * causal_depthwise_conv3(C * u), 512 channels (8 groups of 64)
  y_a = A_out @ W_a, y_b = B_out @ W_b                      (each branch -> D_MODEL)
  x = x + (sigmoid(gate_a) * y_a + sigmoid(gate_b) * y_b) @ W_o
  x = x + PEER(RMSNorm(x))   (product-key retrieval over 128^2 single-neuron experts)
Output: RMSNorm(x).
Inputs: x (BATCH, SEQ, D_MODEL) float32 plus per-layer weights stacked on a leading DEPTH axis.
Output: (BATCH, SEQ, D_MODEL).
'''

D_MODEL = 1024
BATCH = 1
SEQ = 512
DEPTH = 1

CHUNK = 64
QUERY_BLOCK = 2 * CHUNK
SB_HEADS = 8
SB_HEAD_DIM = 64
SB_WIDTH = SB_HEADS * SB_HEAD_DIM
CONV_GROUPS = 8
CONV_WIDTH = D_MODEL // 2
CONV_K = 3
N_BRANCHES = 2
IN_WIDTH = 3 * SB_WIDTH + 3 * CONV_WIDTH + N_BRANCHES * D_MODEL
PEER_HEADS = 8
PEER_QUERY_DIM = 256
PEER_HALF = PEER_QUERY_DIM // 2
N_KEYS = 128
N_EXPERTS = N_KEYS * N_KEYS
PEER_TOPK = 16
PEER_TOKEN_BLOCK = 128
RMS_EPS = 1e-6

kernel_name = 'hybrid_stickbreak_shortconv_peer'

def rms_norm(x, gain):
    x32 = x.astype(jnp.float32)
    y = x32 * lax.rsqrt(jnp.mean(x32 * x32, axis=-1, keepdims=True) + RMS_EPS)
    return (y * gain.astype(jnp.float32)).astype(x.dtype)

def stick_breaking_attention(q, k, v):
    b, h, t, dh = q.shape
    n_blk = t // QUERY_BLOCK
    scale = dh ** -0.5
    k32 = k.astype(jnp.float32)
    v32 = v.astype(jnp.float32)
    q_blocks = q.reshape(b, h, n_blk, QUERY_BLOCK, dh).transpose(2, 0, 1, 3, 4)
    key_pos = jnp.arange(t)

    def one_block(args):
        q_blk, blk = args
        z = jnp.einsum('bhqd,bhkd->bhqk', q_blk.astype(jnp.float32), k32) * scale
        q_pos = blk * QUERY_BLOCK + jnp.arange(QUERY_BLOCK)
        mask = key_pos[None, :] < q_pos[:, None]
        log_1m_beta = jnp.where(mask, jax.nn.log_sigmoid(-z), 0.0)
        stick = lax.cumsum(log_1m_beta, axis=3, reverse=True) - log_1m_beta
        att = jnp.where(mask, jnp.exp(jax.nn.log_sigmoid(z) + stick), 0.0)
        return jnp.einsum('bhqk,bhkd->bhqd', att, v32)

    out = lax.map(one_block, (q_blocks, jnp.arange(n_blk)))
    return out.transpose(1, 2, 0, 3, 4).reshape(b, h, t, dh).astype(q.dtype)

def short_conv_mixer(b_gate, c_gate, u, conv_w, conv_b):
    z = c_gate * u
    y = lax.conv_general_dilated(
        z, conv_w.astype(z.dtype), window_strides=(1,), padding=[(CONV_K - 1, 0)],
        dimension_numbers=('NWC', 'WIO', 'NWC'), feature_group_count=CONV_WIDTH)
    return b_gate * (y + conv_b.astype(z.dtype))

def peer_ffn(x, w_q, sub_keys, expert_u, expert_v):
    b, t, d = x.shape
    n_blk = (b * t) // PEER_TOKEN_BLOCK
    x_blocks = x.reshape(n_blk, PEER_TOKEN_BLOCK, d)
    keys32 = sub_keys.astype(jnp.float32)

    def one_block(x_blk):
        n = x_blk.shape[0]
        q = (x_blk @ w_q).reshape(n, PEER_HEADS, 2, PEER_HALF).astype(jnp.float32)
        s = jnp.einsum('nhpc,hpkc->nhpk', q, keys32)
        top_s, top_i = lax.top_k(s, PEER_TOPK)
        cand_s = top_s[:, :, 0, :, None] + top_s[:, :, 1, None, :]
        cand_i = top_i[:, :, 0, :, None] * N_KEYS + top_i[:, :, 1, None, :]
        cand_s = cand_s.reshape(n, PEER_HEADS, PEER_TOPK * PEER_TOPK)
        cand_i = cand_i.reshape(n, PEER_HEADS, PEER_TOPK * PEER_TOPK)
        best_s, best_c = lax.top_k(cand_s, PEER_TOPK)
        expert_idx = jnp.take_along_axis(cand_i, best_c, axis=-1)
        gate = jax.nn.softmax(best_s, axis=-1)
        u_sel = expert_u[expert_idx]
        v_sel = expert_v[expert_idx]
        act = jax.nn.gelu(jnp.einsum('nhkd,nd->nhk', u_sel, x_blk).astype(jnp.float32), approximate=False)
        w = (gate * act).astype(v_sel.dtype)
        return jnp.einsum('nhk,nhkd->nd', w, v_sel)

    return lax.map(one_block, x_blocks).reshape(b, t, d).astype(x.dtype)

def hybrid_layer(x, norm_mix, w_in, conv_w, conv_b, w_branch_a, w_branch_b, w_out,
                 norm_ffn, w_q, sub_keys, expert_u, expert_v):
    b, t, _ = x.shape
    h = rms_norm(x, norm_mix)
    proj = h @ w_in
    o1 = SB_WIDTH
    o2 = 2 * SB_WIDTH
    o3 = 3 * SB_WIDTH
    o4 = o3 + CONV_WIDTH
    o5 = o4 + CONV_WIDTH
    o6 = o5 + CONV_WIDTH
    q, k, v, cb, cc, cu, gate_logits = jnp.split(proj, [o1, o2, o3, o4, o5, o6], axis=-1)

    def heads(a):
        return a.reshape(b, t, SB_HEADS, SB_HEAD_DIM).transpose(0, 2, 1, 3)

    att = stick_breaking_attention(heads(q), heads(k), heads(v))
    y_a = att.transpose(0, 2, 1, 3).reshape(b, t, SB_WIDTH) @ w_branch_a
    y_b = short_conv_mixer(cb, cc, cu, conv_w, conv_b) @ w_branch_b

    g = jax.nn.sigmoid(gate_logits.astype(jnp.float32)).reshape(b, t, N_BRANCHES, D_MODEL)
    merged = (g[:, :, 0, :] * y_a.astype(jnp.float32) + g[:, :, 1, :] * y_b.astype(jnp.float32)).astype(x.dtype)
    x = x + merged @ w_out
    x = x + peer_ffn(rms_norm(x, norm_ffn), w_q, sub_keys, expert_u, expert_v)
    return x

def setup_inputs(seed: int = 0) -> dict:
    key = jax.random.key(seed)
    ks = jax.random.split(key, 16)
    f32 = jnp.float32
    nrm = lambda k, shape, s: jax.random.normal(k, shape, f32) * s
    return {
        'x': nrm(ks[0], (BATCH, SEQ, D_MODEL), 1.0),
        'norm_mix': 1.0 + nrm(ks[1], (DEPTH, D_MODEL), 0.02),
        'w_in': nrm(ks[2], (DEPTH, D_MODEL, IN_WIDTH), D_MODEL ** -0.5),
        'conv_w': nrm(ks[3], (DEPTH, CONV_K, 1, CONV_WIDTH), CONV_K ** -0.5),
        'conv_b': nrm(ks[4], (DEPTH, CONV_WIDTH), 0.01),
        'w_branch_a': nrm(ks[5], (DEPTH, SB_WIDTH, D_MODEL), SB_WIDTH ** -0.5),
        'w_branch_b': nrm(ks[6], (DEPTH, CONV_WIDTH, D_MODEL), CONV_WIDTH ** -0.5),
        'w_out': nrm(ks[7], (DEPTH, D_MODEL, D_MODEL), D_MODEL ** -0.5),
        'norm_ffn': 1.0 + nrm(ks[8], (DEPTH, D_MODEL), 0.02),
        'w_q': nrm(ks[9], (DEPTH, D_MODEL, PEER_HEADS * PEER_QUERY_DIM), D_MODEL ** -0.5),
        'sub_keys': nrm(ks[10], (DEPTH, PEER_HEADS, 2, N_KEYS, PEER_HALF), PEER_HALF ** -0.5),
        'expert_u': nrm(ks[11], (DEPTH, N_EXPERTS, D_MODEL), D_MODEL ** -0.5),
        'expert_v': nrm(ks[12], (DEPTH, N_EXPERTS, D_MODEL), PEER_HEADS ** -0.5),
        'final_norm': 1.0 + nrm(ks[13], (D_MODEL,), 0.02),
    }

def reference(x, norm_mix, w_in, conv_w, conv_b, w_branch_a, w_branch_b, w_out,
              norm_ffn, w_q, sub_keys, expert_u, expert_v, final_norm):
    for layer in range(DEPTH):
        x = hybrid_layer(x, norm_mix[layer], w_in[layer], conv_w[layer], conv_b[layer],
                         w_branch_a[layer], w_branch_b[layer], w_out[layer],
                         norm_ffn[layer], w_q[layer], sub_keys[layer],
                         expert_u[layer], expert_v[layer])
    return rms_norm(x, final_norm)


_drawn_inputs = setup_inputs


def setup_inputs(seed=0):
    import zlib

    import numpy as np

    out = dict(_drawn_inputs(seed))
    spreads = {}
    factors = {'conv_b': 4.98, 'final_norm': 7.535, 'norm_ffn': 2.675}
    for name, (base, spread) in spreads.items():
        noise = np.random.default_rng([zlib.crc32(name.encode()), seed]).standard_normal(out[name].shape)
        drawn = base * np.exp(spread * noise) if base else spread * noise
        out[name] = __import__('jax').numpy.asarray(drawn.astype(out[name].dtype))
    for name, factor in factors.items():
        out[name] = (out[name] * factor).astype(out[name].dtype)
    return out
```

```python
from contextlib import ExitStack

import numpy as np
import concourse.bass as bass
from concourse import mybir

F = mybir.dt.float32
R = mybir.dt.float32r
U32 = mybir.dt.uint32
ALU = mybir.AluOpType
ACT = mybir.ActivationFunctionType
X = mybir.AxisListType.X
ds = bass.ds

P = 128
T = 512
D = 1024
NB = T // P
C = D // P
SBW = 512
CW = 512
HEADS = 8
PAIRS = HEADS // 2
HD = 64
CT = CW // P
KEYS = 128
LISTS = 16
TOPK = 16
EPS = 1e-6
NEG = -3.0e38
FAR = -1.0e30
KB = 1024
PRIMED = 1

Q0, K0, V0 = 0, SBW, 2 * SBW
CB0, CC0, CU0 = 3 * SBW, 3 * SBW + CW, 3 * SBW + 2 * CW
GA0 = 3 * SBW + 3 * CW
GB0 = GA0 + D

OFF = {0: (512, 384), 2: (896, 128), 1: (1024, 256)}
ZW = 1280


class Map:

    def __init__(self, nc, base):
        self.nc, self.base = nc, base

    def put(self, name, kb, shape, dt=F):
        return self.nc.alloc_sbuf_tensor_at(name, shape, dt, offset=self.base + int(kb * KB))


def mix_program(nc, sem, psum, m, a, acc, sT, const):
    ident, iota, tri, ones, causal, gap, vecs = (const[k] for k in (
        "ident", "iota", "tri", "ones", "causal", "gap", "vecs"))
    xh, xl = sT
    score = m.put("score", 52, [P, NB, LISTS, KEYS])
    ath = m.put("ath", 52, [P, PAIRS, T], R)
    atl = m.put("atl", 60, [P, PAIRS, T], R)
    cvh = m.put("cvh", 68, [P, CT, T], R)
    cvl = m.put("cvl", 76, [P, CT, T], R)
    mgh = m.put("mgh", 84, [P, C, T], R)
    mgl = m.put("mgl", 100, [P, C, T], R)
    xn = m.put("xn", 84, [P, NB, D])
    raw = [m.put(f"raw{i}", 116 + 4 * i, [P, C, P]) for i in range(3)]
    wh = [m.put(f"wh{i}", 128 + 4 * i, [P, C, P], R) for i in range(3)]
    wl = [m.put(f"wl{i}", 140 + 4 * i, [P, C, P], R) for i in range(3)]
    z = m.put("z", 152, [P, 2, ZW])
    sp = m.put("sp", 162, [P, 2, ZW])
    qT = m.put("qT", 172, [P, T])
    kT = m.put("kT", 174, [P, T])
    vT = m.put("vT", 176, [P, T])
    v = m.put("v", 178, [P, NB, P])
    cb = m.put("cb", 180, [P, T])
    cc = m.put("cc", 182, [P, T])
    cz = m.put("cz", 184, [P, 2 + T])
    cy = m.put("cy", 187, [P, T])
    ga = m.put("ga", 189, [P, T])
    gb = m.put("gb", 191, [P, T])
    ot = [m.put(f"ot{i}", 193 + 2 * i, [P, T]) for i in range(2)]
    keyT = m.put("keyT", 152, [P, LISTS, KEYS])
    key = m.put("key", 160, [P, LISTS, P])
    rows = m.put("rows", 197, [32, P])
    zeros = m.put("zeros", 199, [P, P])
    count = m.put("count", 199.5, [P, P], U32)
    st = m.put("st", 198, [P, 4, NB])
    ss, var, rs, tmp = (st[:, i, :] for i in range(4))

    pj = psum[0:3]
    zt = psum[3:6]
    av = psum[6]
    tp = psum[7]

    S = {n: sem(n) for n in (
        "x_in rows_in key_in sq_done var_ready root_ready xn_ready vec_T vec_in xT_full xT_hi xT_lo "
        "vT_full v_ready z_full z_copied abs_done soft_done sp_ready t_full "
        "t_used arg_ready att_ready av_full av_hi av_lo cv_y cv_hi cv_lo "
        "mg_sum mg_hi mg_lo oT_full x_added "
        "key_T key_ready s_full s_out consts vchain vmax conv wcol made raw_b").split()}
    raw_in = [sem(f"raw_in{i}") for i in range(3)]
    w_hi = [sem(f"w_hi{i}") for i in range(3)]
    w_lo = [sem(f"w_lo{i}") for i in range(3)]
    tile_done = [sem(f"tile_done{i}") for i in range(3)]
    taken = [sem(f"taken{i}") for i in range(3)]

    w_in = a["w_in"][0].rearrange("(c p) f -> p c f", p=P)
    w_q = a["w_q"][0].rearrange("(c p) f -> p c f", p=P)
    w_o = a["w_out"][0].rearrange("(c p) f -> p c f", p=P)
    w_a = a["w_branch_a"][0].rearrange("(c p) f -> p c f", p=P)
    w_b = a["w_branch_b"][0].rearrange("(c p) f -> p c f", p=P)
    L4 = 16

    with nc.Block() as block:
        @block.sync
        def _(sp_):
            for free in (*w_lo, *(S[n] for n in ("t_used", "av_lo", "x_added", "s_out", "oT_full", "s_full"))):
                sp_.sem_inc(free, PRIMED)
            sp_.dma_start(acc[:], a["x"][0].rearrange("(b p) d -> p b d", p=P)).then_inc(S["x_in"], 16)
            for r0, n, src in ((0, C, a["norm_mix"][0].rearrange("(c p) -> c p", p=P)),
                               (8, C, a["norm_ffn"][0].rearrange("(c p) -> c p", p=P)),
                               (16, 12, a["conv_w"][0].rearrange("k o (t p) -> (k o t) p", p=P)),
                               (28, CT, a["conv_b"][0].rearrange("(t p) -> t p", p=P))):
                sp_.dma_start(rows[r0:r0 + n, :], src).then_inc(S["rows_in"], 16)

            def load(slot, r, src):
                sp_.wait_ge(S["x_in"], 16)
                sp_.wait_ge(w_lo[slot], r + PRIMED)
                n = src.shape[1]
                sp_.dma_start(raw[slot][:, 0:n, :], src).then_inc(raw_in[slot], 16)

            with sp_.Fori(0, PAIRS) as p:
                for slot, f0 in enumerate((Q0, K0, V0)):
                    load(slot, p, w_in[:, :, ds(p * P + f0, P)])
            with sp_.Fori(0, CT) as t:
                for slot, f0 in enumerate((CB0, CC0, CU0)):
                    load(slot, t + PAIRS, w_in[:, :, ds(t * P + f0, P)])
            with sp_.Fori(0, C) as c:
                load(0, c + 8, w_in[:, :, ds(c * P + GA0, P)])
                load(1, c + 8, w_in[:, :, ds(c * P + GB0, P)])
                load(2, c + 8, w_a[:, :, ds(c * P, P)])
                sp_.dma_start(raw[2][:, 4:8, :], w_b[:, :, ds(c * P, P)]).then_inc(S["raw_b"], 16)
            with sp_.Fori(0, C // 2) as i:
                for slot in range(2):
                    load(slot, i + L4, w_o[:, :, ds(i * 2 * P + slot * P, P)])
            sp_.wait_ge(S["av_hi"], PAIRS)
            sp_.dma_start(key[:], a["sub_keys"][0].rearrange("h q k c -> k (h q) c")).then_inc(S["key_in"], 16)
            with sp_.Fori(0, LISTS // 2) as i:
                for slot in range(2):
                    load(slot, i + (L4 + C // 2), w_q[:, :, ds(i * 2 * P + slot * P, P)])

        @block.gpsimd
        def _(pool):
            nc.gpsimd.memset(ones[:], 1.0)
            nc.gpsimd.memset(zeros[:], 0.0)
            nc.gpsimd.iota(count[:], pattern=[[1, P]], base=0, channel_multiplier=0).then_inc(S["made"], 1)
            pool.wait_ge(S["made"], 1)
            nc.gpsimd.tensor_copy(iota[:], count[:])
            for out_, in_, op, fill, step, per in (
                    (ident, zeros, ALU.not_equal, 1.0, -1, 1),
                    (tri, ones, ALU.is_ge, 0.0, -1, 1),
                    (causal, ones, ALU.is_gt, 0.0, 1, -1),
                    (gap, zeros, ALU.is_gt, FAR, 1, -1)):
                last = nc.gpsimd.affine_select(out=out_[:], in_=in_[:], compare_op=op, fill=fill, base=0,
                                               pattern=[[step, P]], channel_multiplier=per)
            last.then_inc(S["consts"], 1)

            def split(slot, r):
                pool.wait_ge(w_hi[slot], r + 1)
                nc.gpsimd.tensor_tensor(wl[slot][:], raw[slot][:], wh[slot][:].bitcast(F),
                                        ALU.subtract).then_inc(w_lo[slot], 1)

            with pool.Fori(0, PAIRS + CT) as r:
                for slot in range(3):
                    split(slot, r)
            with pool.Fori(0, C) as c:
                for slot in range(3):
                    split(slot, c + (PAIRS + CT))
            with pool.Fori(L4, L4 + 12) as r:
                for slot in range(2):
                    split(slot, r)

        @block.tensor
        def _(pe):
            def three_pass(out, slot, hi, lo, chunks, w0=0):
                for i in range(chunks):
                    for n, (w, x) in enumerate(((wh, hi), (wh, lo), (wl, hi))):
                        last = nc.tensor.matmul(out, w[slot][:, w0 + i, :], x[:, i, :],
                                                start=(i == 0 and n == 0), stop=(i == chunks - 1 and n == 2))
                return last

            def project(slot, r, hi, lo):
                pe.wait_ge(w_lo[slot], r + 1 + PRIMED)
                pe.wait_ge(taken[slot], r)
                three_pass(pj[slot][:], slot, hi, lo, C).then_inc(tile_done[slot], 1)

            def norm_transposes(first, n0):
                pe.wait_ge(S["xn_ready"], n0)
                for c in range(C):
                    pe.wait_ge(S["xT_lo"], first + c)
                    for b in range(NB):
                        last = nc.tensor.transpose(tp[:, b * P:(b + 1) * P], xn[:, b, c * P:(c + 1) * P], ident[:])
                    last.then_inc(S["xT_full"], 1)

            def scores(p):
                pe.wait_ge(taken[1], p + 1)
                for e in range(2):
                    h = slice(e * HD, (e + 1) * HD)
                    pe.wait_ge(S["t_used"], p * 2 + PRIMED)
                    if e:
                        pe.wait_ge(S["z_copied"], p * 2 + 1)
                    for b in range(NB):
                        nc.tensor.matmul(zt[0][:, b * P:(b + 1) * P], kT[h, b * P:(b + 1) * P],
                                         qT[h, b * P:(b + 1) * P], start=True, stop=True)
                    for kb, (o, n) in OFF.items():
                        last = nc.tensor.matmul(zt[o // T][:, o % T:o % T + n], kT[h, kb * P:(kb + 1) * P],
                                                qT[h, (kb + 1) * P:], start=True, stop=True)
                    last.then_inc(S["z_full"], 1)

            def sums(p):
                for e in range(2):
                    pe.wait_ge(S["sp_ready"], p * 2 + e + 1)
                    pe.wait_ge(S["z_copied"], p * 2 + 2)
                    pe.wait_ge(S["t_used"], p * 2 + e + PRIMED)
                    for b in range(NB):
                        nc.tensor.matmul(zt[0][:, b * P:(b + 1) * P], tri[:], sp[:, e, b * P:(b + 1) * P],
                                         start=True, stop=True)
                    for kb, (o, n) in OFF.items():
                        bank, o0 = zt[o // T], o % T
                        parts = [(tri, o, n, o0)]
                        for jb in range(kb + 1, NB):
                            at = o0 + (jb - kb - 1) * P
                            parts.append((ones, jb * P, P, at))
                            if jb < NB - 1:
                                parts.append((ones, OFF[jb][0], OFF[jb][1], at + P))
                        for n_, (w, src, width, at) in enumerate(parts):
                            last = nc.tensor.matmul(bank[:, at:at + width], w[:], sp[:, e, src:src + width],
                                                    start=(n_ == 0), stop=(n_ == len(parts) - 1))
                    last.then_inc(S["t_full"], 1)

            def outputs(p):
                pe.wait_ge(S["av_lo"], p + PRIMED)
                pe.wait_ge(S["v_ready"], p + 1)
                for e in range(2):
                    h = slice(e * HD, (e + 1) * HD)
                    pe.wait_ge(S["att_ready"], p * 2 + e + 1)
                    parts = [(kb, *OFF[kb], (kb + 1) * P) for kb in (0, 1, 2)] + [(b, b * P, P, b * P) for b in range(NB)]
                    for n_, (kb, src, width, at) in enumerate(parts):
                        last = nc.tensor.matmul(av[h, at:at + width], v[:, kb, h], z[:, e, src:src + width],
                                                start=(n_ == 0), stop=(n_ == len(parts) - 1))
                last.then_inc(S["av_full"], 1)

            def transpose_v(p):
                pe.wait_ge(taken[2], p + 1)
                for b in range(NB):
                    last = nc.tensor.transpose(tp[:, b * P:(b + 1) * P], vT[:, b * P:(b + 1) * P], ident[:])
                last.then_inc(S["vT_full"], 1)

            pe.wait_ge(S["consts"], 1)
            pe.wait_ge(S["rows_in"], 64)
            nc.tensor.transpose(pj[0][:, 0:32], rows[:, :], ident[0:32, 0:32]).then_inc(S["vec_T"], 1)
            norm_transposes(0, NB)
            pe.wait_ge(S["xT_lo"], C)
            pe.wait_ge(S["vec_in"], 1)
            for slot in range(3):
                project(slot, 0, xh, xl)
            transpose_v(0)
            with pe.Fori(1, PAIRS) as p:
                scores(p - 1)
                project(0, p, xh, xl)
                sums(p - 1)
                project(1, p, xh, xl)
                outputs(p - 1)
                project(2, p, xh, xl)
                transpose_v(p)
            scores(PAIRS - 1)
            project(0, PAIRS, xh, xl)
            sums(PAIRS - 1)
            project(1, PAIRS, xh, xl)
            outputs(PAIRS - 1)
            project(2, PAIRS, xh, xl)
            with pe.Fori(PAIRS + 1, PAIRS + CT) as r:
                for slot in range(3):
                    project(slot, r, xh, xl)
            with pe.Fori(PAIRS + CT, L4) as r:
                project(0, r, xh, xl)
                project(1, r, xh, xl)
                pe.wait_ge(S["av_lo"], PAIRS + PRIMED)
                pe.wait_ge(S["cv_lo"], CT)
                pe.wait_ge(w_lo[2], r + 1 + PRIMED)
                pe.wait_ge(taken[2], r)
                three_pass(pj[2][:], 2, ath, atl, 4)
                three_pass(zt[0][:], 2, cvh, cvl, 4, w0=4).then_inc(tile_done[2], 1)
            pe.wait_ge(S["mg_lo"], C)
            with pe.Fori(0, C // 2) as i:
                for slot in range(2):
                    project(slot, i + L4, mgh, mgl)
                for slot in range(2):
                    pe.wait_ge(taken[slot], i + (L4 + 1))
                    pe.wait_ge(S["x_added"], i * 2 + slot + PRIMED)
                    for b in range(NB):
                        last = nc.tensor.transpose(tp[:, b * P:(b + 1) * P], ot[slot][:, b * P:(b + 1) * P], ident[:])
                    last.then_inc(S["oT_full"], 1)
            pe.wait_ge(S["key_in"], 16)
            for g in range(LISTS // 4):
                pe.wait_ge(S["key_ready"], g)
                for q in range(4):
                    last = nc.tensor.transpose(zt[1][:, q * P:(q + 1) * P], key[:, 4 * g + q, :], ident[:])
                last.then_inc(S["key_T"], 1)
            norm_transposes(C, 2 * NB)
            pe.wait_ge(S["xT_lo"], 2 * C)
            pe.wait_ge(S["key_ready"], LISTS // 4)
            with pe.Fori(0, LISTS // 2) as i:
                for slot in range(2):
                    project(slot, i + (L4 + C // 2), xh, xl)
                for slot in range(2):
                    pe.wait_ge(taken[slot], i + (L4 + C // 2 + 1))
                    pe.wait_ge(S["s_out"], i * 2 + PRIMED)
                    for b in range(NB):
                        last = nc.tensor.matmul(zt[slot][:, b * P:(b + 1) * P], ot[slot][:, b * P:(b + 1) * P],
                                                keyT[:, ds(i * 2 + slot, 1), :], start=True, stop=True)
                    last.then_inc(S["s_full"], 1)

        @block.scalar
        def _(act):
            def squares(first):
                for b in range(NB):
                    nc.scalar.activation(xn[:, b, :], acc[:, b, :], ACT.Square,
                                         accum_out=ss[:, b:b + 1]).then_inc(S["sq_done"], 1)
                act.wait_ge(S["var_ready"], first + 1)
                nc.scalar.activation(rs, var, ACT.Sqrt).then_inc(S["root_ready"], 1)

            def norm_hi(first, gain):
                for c in range(C):
                    act.wait_ge(S["xT_full"], first + c + 1)
                    nc.scalar.activation(xh[:, c, :], tp[:], ACT.Copy,
                                         scale=vecs[:, gain + c:gain + c + 1]).then_inc(S["xT_hi"], 1)

            def copy_scores(p):
                for e in range(2):
                    act.wait_ge(S["z_full"], p * 2 + e + 1)
                    for b, n in enumerate((T, T, ZW - 2 * T)):
                        last = nc.scalar.activation(z[:, e, b * T:b * T + n], zt[b][:, 0:n], ACT.Copy)
                    last.then_inc(S["z_copied"], 1)

            def softplus(p):
                act.wait_ge(S["abs_done"], p + 1)
                nc.scalar.activation(sp[:], sp[:], ACT.Exp, scale=-1.0).then_inc(S["soft_done"], 1)
                act.wait_ge(S["soft_done"], p * 2 + 1)
                nc.scalar.activation(sp[:], sp[:], ACT.Ln, bias=1.0).then_inc(S["soft_done"], 1)

            def exps(p):
                for e in range(2):
                    act.wait_ge(S["arg_ready"], p * 2 + e + 1)
                    nc.scalar.activation(z[:, e, :], z[:, e, :], ACT.Exp).then_inc(S["att_ready"], 1)

            def attention_hi(p):
                act.wait_ge(S["av_full"], p + 1)
                nc.scalar.activation(ath[:, ds(p, 1), :] if not isinstance(p, int) else ath[:, p:p + 1, :],
                                     av[:], ACT.Copy).then_inc(S["av_hi"], 1)

            def take(slot, r, out, func=ACT.Copy, scale=1.0):
                act.wait_ge(tile_done[slot], r + 1)
                nc.scalar.activation(out, pj[slot][:], func, scale=scale).then_inc(taken[slot], 1)

            def high(slot, r):
                act.wait_ge(raw_in[slot], r * 16 + 16)
                act.wait_ge(tile_done[slot], r)
                nc.scalar.activation(wh[slot][:], raw[slot][:], ACT.Copy).then_inc(w_hi[slot], 1)

            def both_highs(c):
                act.wait_ge(S["raw_b"], c * 16 + 16)
                high(2, c + (PAIRS + CT))

            high(0, 0)
            act.wait_ge(S["x_in"], 16)
            squares(0)
            norm_hi(0, 0)
            high(1, 0)
            take(0, 0, qT[:], scale=HD ** -0.5)
            high(2, 0)
            take(1, 0, kT[:])
            high(0, 1)
            take(2, 0, vT[:])
            with act.Fori(1, PAIRS) as p:
                copy_scores(p - 1)
                high(1, p)
                take(0, p, qT[:], scale=HD ** -0.5)
                softplus(p - 1)
                high(2, p)
                take(1, p, kT[:])
                exps(p - 1)
                high(0, p + 1)
                attention_hi(p - 1)
                take(2, p, vT[:])
            copy_scores(PAIRS - 1)
            high(1, PAIRS)
            take(0, PAIRS, cb[:])
            softplus(PAIRS - 1)
            high(2, PAIRS)
            take(1, PAIRS, cc[:])
            exps(PAIRS - 1)
            high(0, PAIRS + 1)
            attention_hi(PAIRS - 1)

            def conv_hi(t):
                act.wait_ge(S["cv_y"], t + 1)
                nc.scalar.activation(cvh[:, ds(t, 1), :], cy[:], ACT.Copy).then_inc(S["cv_hi"], 1)

            act.wait_ge(S["cv_y"], 1)
            nc.scalar.activation(cvh[:, 0, :], cy[:], ACT.Copy).then_inc(S["cv_hi"], 1)
            with act.Fori(PAIRS + 1, PAIRS + CT) as r:
                high(1, r)
                take(0, r, cb[:])
                high(2, r)
                take(1, r, cc[:])
                high(0, r + 1)
                conv_hi(r - PAIRS)
            with act.Fori(PAIRS + CT, L4) as r:
                high(1, r)
                take(0, r, ga[:], ACT.Sigmoid)
                both_highs(r - (PAIRS + CT))
                take(1, r, gb[:], ACT.Sigmoid)
                high(0, r + 1)
                act.wait_ge(S["mg_sum"], r - (PAIRS + CT) + 1)
                nc.scalar.activation(mgh[:, ds(r - (PAIRS + CT), 1), :], ga[:], ACT.Copy).then_inc(S["mg_hi"], 1)
                act.wait_ge(S["mg_lo"], r - (PAIRS + CT) + 1)
            with act.Fori(0, C // 2) as i:
                for slot in range(2):
                    high(1 - slot, i + (L4 + slot))
                    act.wait_ge(S["oT_full"], i * 2 + PRIMED)
                    take(slot, i + L4, ot[slot][:])
            for g in range(LISTS // 4):
                act.wait_ge(S["key_T"], g + 1)
                nc.scalar.activation(keyT[:, 4 * g:4 * g + 4, :], zt[1][:], ACT.Copy).then_inc(S["key_ready"], 1)
            act.wait_ge(S["x_added"], C + PRIMED)
            squares(1)
            norm_hi(C, C)

            def take_query(i, slot):
                act.wait_ge(S["s_full"], i * 2 + PRIMED)
                take(slot, i + (L4 + C // 2), ot[slot][:])

            with act.Fori(0, LISTS // 2 - 1) as i:
                for slot in range(2):
                    high(1 - slot, i + (L4 + C // 2 + slot))
                    take_query(i, slot)
            high(1, L4 + C // 2 + LISTS // 2 - 1)
            for slot in range(2):
                take_query(LISTS // 2 - 1, slot)

        @block.vector
        def _(dve):
            done = [0]

            def chain(ins):
                done[0] += 1
                ins.then_inc(S["vchain"], 1)
                dve.wait_ge(S["vchain"], done[0])

            def normed(first):
                dve.wait_ge(S["sq_done"], (first + 1) * NB)
                nc.vector.tensor_scalar(var, ss, 1.0 / D, EPS, ALU.mult, ALU.add).then_inc(S["var_ready"], 1)
                dve.wait_ge(S["root_ready"], first + 1)
                chain(nc.vector.reciprocal(rs, rs))
                chain(nc.vector.tensor_tensor(tmp, rs, rs, ALU.mult))
                chain(nc.vector.tensor_tensor(tmp, tmp, var, ALU.mult))
                chain(nc.vector.tensor_scalar(tmp, tmp, -0.5, 1.5, ALU.mult, ALU.add))
                chain(nc.vector.tensor_tensor(rs, rs, tmp, ALU.mult))
                for b in range(NB):
                    nc.vector.tensor_scalar(xn[:, b, :], acc[:, b, :], rs[:, b:b + 1], None,
                                            ALU.mult).then_inc(S["xn_ready"], 1)

            def norm_lo(first, gain):
                for c in range(C):
                    dve.wait_ge(S["xT_hi"], first + c + 1)
                    nc.vector.scalar_tensor_tensor(xl[:, c, :], tp[:], vecs[:, gain + c:gain + c + 1],
                                                   xh[:, c, :].bitcast(F), ALU.mult,
                                                   ALU.subtract).then_inc(S["xT_lo"], 1)

            chain(nc.vector.memset(cz[:, 0:2], 0.0))
            dve.wait_ge(S["vec_T"], 1)
            nc.vector.tensor_copy(vecs[:], pj[0][:, 0:32]).then_inc(S["vec_in"], 1)
            dve.wait_ge(S["vec_in"], 1)
            normed(0)
            norm_lo(0, 0)

            def take_v(p):
                dve.wait_ge(S["vT_full"], p + 1)
                nc.vector.tensor_copy(v[:], tp[:].rearrange("p (b f) -> p b f", b=NB)).then_inc(S["v_ready"], 1)

            diag = lambda x, e: x[:, e, 0:T].rearrange("p (b q) -> p b q", b=NB)
            wide = lambda x: x[:].unsqueeze(1).broadcast_to([P, NB, P])

            def magnitudes(p):
                dve.wait_ge(S["z_copied"], p * 2 + 2)
                nc.vector.scalar_tensor_tensor(sp[:], z[:], -1.0, z[:], ALU.mult, ALU.max).then_inc(S["abs_done"], 1)

            def soft(p):
                for e in range(2):
                    dve.wait_ge(S["soft_done"], p * 2 + 2)
                    nc.vector.scalar_tensor_tensor(sp[:, e, :], z[:, e, :], 0.0, sp[:, e, :], ALU.max,
                                                   ALU.add).then_inc(S["vmax"], 1)
                    dve.wait_ge(S["vmax"], p * 2 + e + 1)
                    nc.vector.tensor_tensor(diag(sp, e), diag(sp, e), wide(causal), ALU.mult).then_inc(S["sp_ready"], 1)

            def arguments(p):
                for e in range(2):
                    dve.wait_ge(S["t_full"], p * 2 + e + 1)
                    for b, n in enumerate((T, T, ZW - 2 * T)):
                        last = nc.vector.tensor_tensor(z[:, e, b * T:b * T + n], z[:, e, b * T:b * T + n],
                                                       zt[b][:, 0:n], ALU.subtract)
                    last.then_inc(S["t_used"], 1)
                    dve.wait_ge(S["t_used"], p * 2 + e + 1 + PRIMED)
                    chained = nc.vector.scalar_tensor_tensor(diag(z, e), diag(z, e), 0.0, wide(gap), ALU.min,
                                                             ALU.add)
                    chained.then_inc(S["arg_ready"], 1)

            def attention_lo(p):
                dve.wait_ge(S["av_hi"], p + 1)
                at = slice(p, p + 1) if isinstance(p, int) else ds(p, 1)
                nc.vector.tensor_tensor(atl[:, at, :], av[:].unsqueeze(1), ath[:, at, :].bitcast(F),
                                        ALU.subtract).then_inc(S["av_lo"], 1)

            take_v(0)
            with dve.Fori(1, PAIRS) as p:
                magnitudes(p - 1)
                soft(p - 1)
                arguments(p - 1)
                attention_lo(p - 1)
                take_v(p)
            magnitudes(PAIRS - 1)
            soft(PAIRS - 1)
            arguments(PAIRS - 1)
            attention_lo(PAIRS - 1)

            wcol = m.put("wcol", 198.5, [P, 4])

            def convolve(t):
                def step(n, ins):
                    ins.then_inc(S["conv"], 1)
                    dve.wait_ge(S["conv"], t * 3 + n)
                cols = vecs[:, 16:32].rearrange("p (k t) -> p k t", k=4)
                at = slice(t, t + 1) if isinstance(t, int) else ds(t, 1)
                nc.vector.tensor_copy(wcol[:].unsqueeze(2), cols[:, :, at]).then_inc(S["wcol"], 1)
                dve.wait_ge(S["wcol"], t + 1)
                dve.wait_ge(taken[1], t + (PAIRS + 1))
                dve.wait_ge(tile_done[2], t + (PAIRS + 1))
                nc.vector.tensor_tensor(cz[:, 2:2 + T], pj[2][:], cc[:], ALU.mult).then_inc(taken[2], 1)
                dve.wait_ge(taken[2], t + (PAIRS + 1))
                step(1, nc.vector.tensor_scalar(cy[:], cz[:, 2:2 + T], wcol[:, 2:3], wcol[:, 3:4], ALU.mult, ALU.add))
                step(2, nc.vector.scalar_tensor_tensor(cy[:], cz[:, 1:1 + T], wcol[:, 1:2], cy[:], ALU.mult, ALU.add))
                step(3, nc.vector.scalar_tensor_tensor(cy[:], cz[:, 0:T], wcol[:, 0:1], cy[:], ALU.mult, ALU.add))
                nc.vector.tensor_tensor(cy[:], cy[:], cb[:], ALU.mult).then_inc(S["cv_y"], 1)
                dve.wait_ge(S["cv_hi"], t + 1)
                nc.vector.tensor_tensor(cvl[:, at, :], cy[:].unsqueeze(1), cvh[:, at, :].bitcast(F),
                                        ALU.subtract).then_inc(S["cv_lo"], 1)

            convolve(0)
            with dve.Fori(1, CT) as t:
                convolve(t)

            with dve.Fori(0, C) as c:
                dve.wait_ge(taken[1], c + (PAIRS + CT + 1))
                dve.wait_ge(tile_done[2], c + (PAIRS + CT + 1))
                nc.vector.tensor_tensor(gb[:], gb[:], zt[0][:], ALU.mult)
                nc.vector.tensor_tensor(ga[:], ga[:], pj[2][:], ALU.mult).then_inc(taken[2], 1)
                dve.wait_ge(taken[2], c + (PAIRS + CT + 1))
                nc.vector.tensor_tensor(ga[:], ga[:], gb[:], ALU.add).then_inc(S["mg_sum"], 1)
                dve.wait_ge(S["mg_hi"], c + 1)
                nc.vector.tensor_tensor(mgl[:, ds(c, 1), :], ga[:].unsqueeze(1), mgh[:, ds(c, 1), :].bitcast(F),
                                        ALU.subtract).then_inc(S["mg_lo"], 1)

            with dve.Fori(0, C) as c:
                dve.wait_ge(S["oT_full"], c + 1 + PRIMED)
                part = acc[:, :, ds(c * P, P)]
                nc.vector.tensor_tensor(part, part, tp[:].rearrange("p (b f) -> p b f", b=NB),
                                        ALU.add).then_inc(S["x_added"], 1)
            normed(1)
            norm_lo(C, C)
            with dve.Fori(0, LISTS // 2) as i:
                for slot in range(2):
                    dve.wait_ge(S["s_full"], i * 2 + slot + 1 + PRIMED)
                    nc.vector.tensor_copy(score[:, :, ds(i * 2 + slot, 1), :],
                                          zt[slot][:].rearrange("p (b o k) -> p b o k", b=NB, o=1)).then_inc(S["s_out"], 1)
    return score


def up_program(nc, sem, psum, m, a, sT, const, score, hd, gd):
    ident, iota = const["ident"], const["iota"]
    xh, xl = sT
    raw = [m.put(f"u_raw{i}", 84 + 4 * i, [P, D]) for i in range(2)]
    uh = [m.put(f"uh{i}", 92 + 4 * i, [P, C, P], R) for i in range(2)]
    ul = [m.put(f"ul{i}", 100 + 4 * i, [P, C, P], R) for i in range(2)]
    hb = [m.put(f"hb{i}", 108 + 2 * i, [P, T]) for i in range(2)]
    grid = [m.put(f"grid{i}", 112 + 16 * i, [P, KEYS, 32]) for i in range(2)]
    lists = m.put("lists", 144, [P, 2, KEYS])
    left = m.put("left", 145, [P, KEYS])
    top = m.put("top", 145.5, [P, 2, TOPK])
    cand = m.put("cand", 146, [P, TOPK, TOPK])
    cleft = m.put("cleft", 147, [P, TOPK, TOPK])
    best = m.put("best", 148, [P, TOPK])
    picks = m.put("picks", 148.5, [P, 4, TOPK], U32)
    pos = m.put("pos", 149, [P, TOPK], U32)
    best_all = m.put("best_all", 150, [P, NB * HEADS, TOPK])
    picks_all = m.put("picks_all", 152, [P, NB * HEADS, 4, TOPK])
    sel = m.put("sel", 160, [P, 3, HEADS * TOPK])
    peak = m.put("peak", 162, [P, 2, HEADS])
    selT = m.put("selT", 163, [P, 3, T])
    eq = [m.put(f"eq{i}", 170 + 8 * i, [P, HEADS * TOPK, TOPK]) for i in range(2)]
    hot = [m.put(f"hot{i}", 186 + 8 * i, [P, 8, 2, KEYS]) for i in range(2)]

    utp = [psum[0:2], psum[2:4]]
    zb = psum[4:6]
    gp = psum[6:8]

    u_in, ut_full, ut_hi, ut_lo, u_mm, h_done, h_out, hot_ready, g_full, g_out = (
        [sem(f"{n}{i}") for i in range(2)] for n in (
            "u_in", "ut_full", "ut_hi", "ut_lo", "u_mm", "h_done", "h_out", "hot_ready", "g_full", "g_out"))
    S = {n: sem(n) for n in ("pick picked sel_in exp_in exp_out sel_ready selT_full selT_in "
                             "l2_chain g_evac").split()}
    eq_hot, eq_key = [sem(f"eq_hot{i}") for i in range(2)], [sem(f"eq_key{i}") for i in range(2)]
    u_view = a["expert_u"][0].rearrange("(i j) d -> i j d", j=KEYS)
    hv = hd.rearrange("i (r s) t -> i r s t", s=2)
    uv = u_view.rearrange("i (r s) d -> i r s d", s=2)

    N1, N2, N3, N4 = 16, NB, 32, 12
    assert N1 + N2 + N3 + N4 == KEYS // 2

    with nc.Block() as block:
        @block.sync
        def _(sp_):
            for free in (*ut_full, *ut_lo, *h_done, *u_mm, *g_full, *(S[n] for n in ("selT_in", "g_evac", "selT_full"))):
                sp_.sem_inc(free, PRIMED)
            for free in (*h_out, *g_out):
                sp_.sem_inc(free, PRIMED * 16)
            with sp_.Fori(0, KEYS // 2) as r:
                for s in range(2):
                    sp_.wait_ge(ut_full[s], r + PRIMED)
                    sp_.dma_start(raw[s][:].unsqueeze(1), uv[:, ds(r, 1), s, :]).then_inc(u_in[s], 16)

        @block.tensor
        def _(pe):
            def transposes(s, r):
                pe.wait_ge(u_in[s], r * 16 + 16)
                pe.wait_ge(ut_lo[s], r + PRIMED)
                for c in range(C):
                    last = nc.tensor.transpose(utp[s][c // 4][:, c % 4 * P:(c % 4 + 1) * P],
                                               raw[s][:, c * P:(c + 1) * P], ident[:])
                last.then_inc(ut_full[s], 1)

            def products(s, r):
                pe.wait_ge(ut_lo[s], r + 1 + PRIMED)
                pe.wait_ge(h_done[s], r + PRIMED)
                for c in range(C):
                    for n, (w, x) in enumerate(((uh, xh), (uh, xl), (ul, xh))):
                        last = nc.tensor.matmul(zb[s][:], w[s][:, c, :], x[:, c, :],
                                                start=(c == 0 and n == 0), stop=(c == C - 1 and n == 2))
                last.then_inc(u_mm[s], 1)

            def step(s, r, ahead=True):
                if ahead:
                    transposes(1 - s, r + s)
                products(s, r)

            def spread(s, r, k):
                pe.wait_ge(hot_ready[s], r + 1)
                pe.wait_ge(S["g_evac"], k + PRIMED)
                for n in range(8):
                    last = nc.tensor.matmul(gp[n // 4][:, n % 4 * P:(n % 4 + 1) * P], hot[s][:, n, 0, :],
                                            hot[s][:, n, 1, :], start=True, stop=True)
                last.then_inc(g_full[s], 1)

            transposes(0, 0)
            with pe.Fori(0, N1) as r:
                for s in range(2):
                    step(s, r)
            with pe.Fori(0, N2) as b:
                for s in range(2):
                    step(s, b + N1)
                pe.wait_ge(S["sel_ready"], b * 2 + 2)
                pe.wait_ge(S["selT_in"], b + PRIMED)
                for n in range(3):
                    last = nc.tensor.transpose(gp[0][:, n * P:(n + 1) * P], sel[:, n, :], ident[:])
                last.then_inc(S["selT_full"], 1)
            with pe.Fori(0, N3 // 4) as q:
                for j in range(8):
                    step(j % 2, q * 4 + (N1 + N2 + j // 2))
                    spread(j % 2, q * 4 + j // 2, q * 8 + j)
            with pe.Fori(N1 + N2 + N3, KEYS // 2 - 1) as r:
                for s in range(2):
                    step(s, r)
            step(0, KEYS // 2 - 1)
            step(1, KEYS // 2 - 1, ahead=False)

        @block.scalar
        def _(act):
            def high(s, r):
                act.wait_ge(ut_full[s], r + 1 + PRIMED)
                act.wait_ge(u_mm[s], r + PRIMED)
                for g in range(2):
                    last = nc.scalar.activation(uh[s][:, 4 * g:4 * g + 4, :], utp[s][g][:], ACT.Copy)
                last.then_inc(ut_hi[s], 1)

            def gelu(s, r):
                act.wait_ge(u_mm[s], r + 1 + PRIMED)
                act.wait_ge(h_out[s], r * 16 + PRIMED * 16)
                nc.scalar.activation(hb[s][:], zb[s][:], ACT.Gelu).then_inc(h_done[s], 1)
                act.wait_ge(h_done[s], r + 1 + PRIMED)
                at = slice(r, r + 1) if isinstance(r, int) else ds(r, 1)
                act.dma_start(hv[:, at, s, :], hb[s][:].unsqueeze(1)).then_inc(h_out[s], 16)

            def step(s, r, ahead=True):
                if ahead:
                    high(1 - s, r + s)
                gelu(s, r)

            high(0, 0)
            with act.Fori(0, N1) as r:
                for s in range(2):
                    step(s, r)
            with act.Fori(0, N2) as b:
                high(1, b + N1)
                act.wait_ge(S["exp_in"], b + 1)
                nc.scalar.activation(sel[:, 2, :], sel[:, 2, :], ACT.Exp).then_inc(S["exp_out"], 1)
                gelu(0, b + N1)
                step(1, b + N1)
            with act.Fori(0, N3 // 4) as q:
                for j in range(8):
                    step(j % 2, q * 4 + (N1 + N2 + j // 2))
                    half, n0 = j // 4, j % 4 * 8
                    act.wait_ge(g_full[j % 2], q * 4 + (j // 2 + 1) + PRIMED)
                    if j % 4 == 0:
                        act.wait_ge(g_out[half], q * 16 + PRIMED * 16)
                    for g in range(2):
                        last = nc.scalar.activation(
                            grid[half][:, :, n0 + 4 * g:n0 + 4 * g + 4].rearrange("p j n -> p n j"),
                            gp[g][:].rearrange("p (n j) -> p n j", n=4), ACT.Copy)
                    last.then_inc(S["g_evac"], 1)
                    if j % 4 == 3:
                        act.wait_ge(S["g_evac"], q * 8 + j + 1 + PRIMED)
                        act.dma_start(gd[:, :, :].rearrange("b p x -> p b x")[:, ds(q * 2 + half, 1), :],
                                      grid[half][:].rearrange("p j n -> p (j n)").unsqueeze(1)).then_inc(g_out[half], 16)
            with act.Fori(N1 + N2 + N3, KEYS // 2 - 1) as r:
                for s in range(2):
                    step(s, r)
            step(0, KEYS // 2 - 1)
            step(1, KEYS // 2 - 1, ahead=False)
            for s in range(2):
                act.wait_ge(h_out[s], KEYS // 2 * 16 + PRIMED * 16)
                act.wait_ge(g_out[s], N3 // 4 * 16 + PRIMED * 16)

        @block.gpsimd
        def _(pool):
            with pool.Fori(0, NB) as b:
                for n in range(2):
                    pool.wait_ge(eq_hot[n], b + 1)
                    view = eq[n][:].rearrange("p (h k) x -> p h k x", h=HEADS)
                    keys = picks_all[:, ds(b * HEADS, HEADS), 2 + n, :].unsqueeze(2)
                    nc.gpsimd.tensor_tensor(view, view, keys.broadcast_to([P, HEADS, TOPK, TOPK]),
                                            ALU.mult).then_inc(eq_key[n], 1)

        @block.vector
        def _(dve):
            def low(s, r):
                dve.wait_ge(ut_hi[s], r + 1)
                for g in range(2):
                    last = nc.vector.tensor_tensor(ul[s][:, 4 * g:4 * g + 4, :].rearrange("p c f -> p (c f)"), utp[s][g][:],
                                                   uh[s][:, 4 * g:4 * g + 4, :].rearrange("p c f -> p (c f)").bitcast(F), ALU.subtract)
                last.then_inc(ut_lo[s], 1)

            def pick(u):
                n = [0]
                dve.sem_clear(S["pick"])

                def step(ins):
                    n[0] += 1
                    ins.then_inc(S["pick"], 1)
                    dve.wait_ge(S["pick"], n[0])

                flat = score[:].rearrange("p b (h q) k -> p (b h) q k", q=2)
                step(nc.vector.tensor_copy(lists[:].unsqueeze(1), flat[:, ds(u, 1), :, :]))
                for q in range(2):
                    t0, t1 = top[:, q, 0:8], top[:, q, 8:16]
                    step(nc.vector.max(t0, lists[:, q, :]))
                    nc.vector.max_index(picks[:, 2 + q, 0:8], t0, lists[:, q, :])
                    step(nc.vector.match_replace(left[:], t0, lists[:, q, :], NEG))
                    step(nc.vector.max(t1, left[:]))
                    step(nc.vector.max_index(picks[:, 2 + q, 8:16], t1, left[:]))
                step(nc.vector.tensor_tensor(cand[:], top[:, 0, :].unsqueeze(2).broadcast_to([P, TOPK, TOPK]),
                                             top[:, 1, :].unsqueeze(1).broadcast_to([P, TOPK, TOPK]), ALU.add))
                flat_c, flat_l = (t[:].rearrange("p x y -> p (x y)") for t in (cand, cleft))
                step(nc.vector.max(best[:, 0:8], flat_c))
                nc.vector.max_index(pos[:, 0:8], best[:, 0:8], flat_c)
                step(nc.vector.match_replace(flat_l, best[:, 0:8], flat_c, NEG))
                step(nc.vector.max(best[:, 8:16], flat_l))
                step(nc.vector.max_index(pos[:, 8:16], best[:, 8:16], flat_l))
                nc.vector.tensor_single_scalar(picks[:, 0, :], pos[:], 4, ALU.logical_shift_right)
                step(nc.vector.tensor_single_scalar(picks[:, 1, :], pos[:], TOPK - 1, ALU.bitwise_and))
                step(nc.vector.tensor_copy(picks_all[:, ds(u, 1), :, :], picks[:].unsqueeze(1)))
                nc.vector.tensor_copy(best_all[:, ds(u, 1), :], best[:].unsqueeze(1)).then_inc(S["picked"], 1)
                dve.wait_ge(S["picked"], u + 1)

            low(0, 0)
            with dve.Fori(0, N1) as r:
                for s in range(2):
                    low(1 - s, r + s)
                    pick(r * 2 + s)
            with dve.Fori(0, N2) as b:
                n = [0]

                def step(ins):
                    n[0] += 1
                    ins.then_inc(S["l2_chain"], 1)
                    dve.wait_ge(S["l2_chain"], b * 3 + n[0])

                scores = best_all[:, ds(b * HEADS, HEADS), :]
                gates = sel[:, 2, :].rearrange("p (h k) -> p h k", h=HEADS)
                dve.wait_ge(S["selT_full"], b + PRIMED)
                nc.vector.tensor_tensor(gates, scores, best_all[:, ds(b * HEADS, HEADS), 0:1].broadcast_to([P, HEADS, TOPK]),
                                        ALU.subtract).then_inc(S["exp_in"], 1)
                low(1, b + N1)
                for q in range(2):
                    place = picks_all[:, ds(b * HEADS, HEADS), q, :].unsqueeze(3)
                    nc.vector.tensor_tensor(
                        eq[q][:].rearrange("p (h k) x -> p h k x", h=HEADS),
                        place.broadcast_to([P, HEADS, TOPK, TOPK]),
                        iota[:, 0:TOPK].unsqueeze(1).unsqueeze(1).broadcast_to([P, HEADS, TOPK, TOPK]),
                        ALU.is_equal).then_inc(eq_hot[q], 1)
                dve.wait_ge(S["exp_out"], b + 1)
                step(nc.vector.tensor_reduce(peak[:, 0, :], gates, X, ALU.add))
                step(nc.vector.reciprocal(peak[:, 1, :], peak[:, 0, :]))
                step(nc.vector.tensor_tensor(gates, gates, peak[:, 1, :].unsqueeze(2).broadcast_to([P, HEADS, TOPK]), ALU.mult))
                for q in range(2):
                    dve.wait_ge(eq_key[q], b + 1)
                    nc.vector.tensor_reduce(sel[:, q, :], eq[q][:], X, ALU.add).then_inc(S["sel_ready"], 1)
                low(0, b + (N1 + 1))
                dve.wait_ge(S["selT_full"], b + 1 + PRIMED)
                nc.vector.tensor_copy(selT[:, :, ds(b * P, P)],
                                      gp[0][:, 0:3 * P].rearrange("p (n t) -> p n t", n=3)).then_inc(S["selT_in"], 1)
            dve.wait_ge(S["selT_in"], NB + PRIMED)
            with dve.Fori(0, N3 // 4) as q:
                for j in range(8):
                    s = j % 2
                    low(1 - s, q * 4 + (N1 + N2 + j // 2 + s))
                    dve.wait_ge(g_full[s], q * 4 + j // 2 + PRIMED)
                    for n in range(8):
                        t = q * 64 + (8 * j + n)
                        nc.vector.tensor_scalar(hot[s][:, n, 0, :], iota[:], selT[:, 0, ds(t, 1)], None, ALU.is_equal)
                        last = nc.vector.tensor_scalar(hot[s][:, n, 1, :], iota[:], selT[:, 1, ds(t, 1)],
                                                       selT[:, 2, ds(t, 1)], ALU.is_equal, ALU.mult)
                    last.then_inc(hot_ready[s], 1)
            with dve.Fori(N1 + N2 + N3, KEYS // 2 - 1) as r:
                for s in range(2):
                    low(1 - s, r + s)
            low(1, KEYS // 2 - 1)


def down_program(nc, sem, psum, m, a, acc, const, hd, gd, out):
    G4 = 4
    ROUNDS = KEYS // G4 // 2
    wh = [m.put(f"dwh{i}", 16 + 8 * i, [P, G4, T], R) for i in range(2)]
    wl = [m.put(f"dwl{i}", 32 + 8 * i, [P, G4, T], R) for i in range(2)]
    raw = [m.put(f"v_raw{i}", 52 + 16 * i, [P, G4, D]) for i in range(2)]
    vh = [m.put(f"vh{i}", 84 + 16 * i, [P, G4, D], R) for i in range(2)]
    vl = [m.put(f"vl{i}", 116 + 16 * i, [P, G4, D], R) for i in range(2)]
    hb = [m.put(f"dh{i}", 148 + 8 * i, [P, G4, T]) for i in range(2)]
    gb = [m.put(f"dg{i}", 164 + 8 * i, [P, T // 32, G4, 32]) for i in range(2)]
    fnorm = m.put("fnorm", 180, [P, D])
    fst = m.put("fst", 184, [P, 4, NB])
    ss, var, rs, tmp = (fst[:, i, :] for i in range(4))
    junk = m.put("junk", 148, [P, NB, D])

    v_in, g_in, h_in, v_hi, v_lo, w_f, w_hi, w_lo, o_full = (
        [sem(f"d_{n}{i}") for i in range(2)] for n in (
            "v_in", "g_in", "h_in", "v_hi", "v_lo", "w_f", "w_hi", "w_lo", "o_full"))
    added = [sem(f"added{k}") for k in range(8)]
    S = {n: sem("d_" + n) for n in "fn_in sq root vchain normed out var".split()}
    vv = a["expert_v"][0].rearrange("(i r j) d -> i r (j d)", r=KEYS // G4, j=G4)
    hv = hd.rearrange("i (r j) t -> i r (j t)", j=G4)
    gv = gd.rearrange("b i (r x) -> i b r x", x=G4 * 32)

    with nc.Block() as block:
        @block.sync
        def _(sp_):
            for free in (*w_lo, *v_lo, *o_full, *added):
                sp_.sem_inc(free, PRIMED)
            sp_.dma_start(fnorm[:], a["final_norm"].unsqueeze(0).broadcast_to([P, D])).then_inc(S["fn_in"], 16)
            with sp_.Fori(0, ROUNDS) as r:
                for s in range(2):
                    g = r * 2 + s
                    sp_.wait_ge(w_lo[s], r + PRIMED)
                    sp_.dma_start(hb[s][:].rearrange("p j t -> p (j t)").unsqueeze(1), hv[:, ds(g, 1), :]).then_inc(h_in[s], 16)
                    sp_.dma_start(gb[s][:].rearrange("p b j n -> p b (j n)"),
                                  gv[:, :, ds(g, 1), :].rearrange("p b o x -> p b (o x)")).then_inc(g_in[s], 16)
                    sp_.wait_ge(v_lo[s], r + PRIMED)
                    sp_.dma_start(raw[s][:].rearrange("p j d -> p (j d)").unsqueeze(1), vv[:, ds(g, 1), :]).then_inc(v_in[s], 16)
            for b in range(NB):
                sp_.wait_ge(S["normed"], b + 1)
                sp_.dma_start(out[0, b * P:(b + 1) * P, :], acc[:, b, :]).then_inc(S["out"], 16)
            sp_.wait_ge(S["out"], NB * 16)

        @block.scalar
        def _(act):
            with act.Fori(0, ROUNDS) as r:
                for s in range(2):
                    act.wait_ge(v_in[s], r * 16 + 16)
                    act.wait_ge(o_full[s], r * 8 + PRIMED)
                    nc.scalar.activation(vh[s][:], raw[s][:], ACT.Copy).then_inc(v_hi[s], 1)
                    act.wait_ge(w_f[s], r + 1)
                    nc.scalar.activation(wh[s][:], hb[s][:], ACT.Copy).then_inc(w_hi[s], 1)
            for k in range(8):
                act.wait_ge(added[k], ROUNDS * 2 + PRIMED)
            for b in range(NB):
                nc.scalar.activation(junk[:, b, :], acc[:, b, :], ACT.Square, accum_out=ss[:, b:b + 1]).then_inc(S["sq"], 1)
            act.wait_ge(S["var"], 1)
            nc.scalar.activation(rs, var, ACT.Sqrt).then_inc(S["root"], 1)

        @block.gpsimd
        def _(pool):
            with pool.Fori(0, ROUNDS) as r:
                for s in range(2):
                    pool.wait_ge(w_hi[s], r + 1)
                    nc.gpsimd.tensor_tensor(wl[s][:], hb[s][:], wh[s][:].bitcast(F), ALU.subtract).then_inc(w_lo[s], 1)

        @block.tensor
        def _(pe):
            with pe.Fori(0, ROUNDS) as r:
                for s in range(2):
                    pe.wait_ge(v_lo[s], r + 1 + PRIMED)
                    pe.wait_ge(w_lo[s], r + 1 + PRIMED)
                    for k in range(8):
                        b, half = k // 2, k % 2
                        pe.wait_ge(added[k], r * 2 + s + PRIMED)
                        for j in range(G4):
                            for n, (w, v) in enumerate(((wh, vh), (wh, vl), (wl, vh))):
                                last = nc.tensor.matmul(psum[k][:], w[s][:, j, b * P:(b + 1) * P],
                                                        v[s][:, j, half * T:(half + 1) * T],
                                                        start=(j == 0 and n == 0), stop=(j == G4 - 1 and n == 2))
                        last.then_inc(o_full[s], 1)

        @block.vector
        def _(dve):
            def prepare(s, r):
                dve.wait_ge(h_in[s], r * 16 + 16)
                dve.wait_ge(g_in[s], r * 16 + 16)
                w = hb[s][:].rearrange("p j (b n) -> p j b n", n=32)
                nc.vector.tensor_tensor(w, w, gb[s][:].rearrange("p b j n -> p j b n"), ALU.mult).then_inc(w_f[s], 1)
                dve.wait_ge(v_hi[s], r + 1)
                nc.vector.tensor_tensor(vl[s][:], raw[s][:], vh[s][:].bitcast(F), ALU.subtract).then_inc(v_lo[s], 1)

            def add(s, r):
                for k in range(8):
                    b, half = k // 2, k % 2
                    dve.wait_ge(o_full[s], r * 8 + (k + 1) + PRIMED)
                    part = acc[:, b, half * T:(half + 1) * T]
                    nc.vector.tensor_tensor(part, part, psum[k][:], ALU.add).then_inc(added[k], 1)

            prepare(0, 0)
            with dve.Fori(0, ROUNDS - 1) as r:
                prepare(1, r)
                add(0, r)
                prepare(0, r + 1)
                add(1, r)
            prepare(1, ROUNDS - 1)
            add(0, ROUNDS - 1)
            add(1, ROUNDS - 1)

            done = [0]

            def chain(ins):
                done[0] += 1
                ins.then_inc(S["vchain"], 1)
                dve.wait_ge(S["vchain"], done[0])

            dve.wait_ge(S["sq"], NB)
            nc.vector.tensor_scalar(var, ss, 1.0 / D, EPS, ALU.mult, ALU.add).then_inc(S["var"], 1)
            dve.wait_ge(S["root"], 1)
            chain(nc.vector.reciprocal(rs, rs))
            chain(nc.vector.tensor_tensor(tmp, rs, rs, ALU.mult))
            chain(nc.vector.tensor_tensor(tmp, tmp, var, ALU.mult))
            chain(nc.vector.tensor_scalar(tmp, tmp, -0.5, 1.5, ALU.mult, ALU.add))
            chain(nc.vector.tensor_tensor(rs, rs, tmp, ALU.mult))
            dve.wait_ge(S["fn_in"], 16)
            for b in range(NB):
                nc.vector.scalar_tensor_tensor(acc[:, b, :], acc[:, b, :], rs[:, b:b + 1], fnorm[:], ALU.mult,
                                               ALU.mult).then_inc(S["normed"], 1)


def layer(nc, a, out):
    ctx = ExitStack()
    with ctx:
        def sem(name):
            return ctx.enter_context(nc.semaphore(name))

        psum = [ctx.enter_context(nc.psum_tensor(f"bank{i}", [P, T], F)) for i in range(8)]
        m = Map(nc, (nc.sbuf_base + 63) // 64 * 64)
        acc = m.put("acc", 0, [P, NB, D])
        sT = m.put("xTh", 16, [P, C, T], R), m.put("xTl", 32, [P, C, T], R)
        const = {n: m.put(n, 48 + i / 2, [P, P])
                 for i, n in enumerate(("ident", "iota", "tri", "ones", "causal", "gap"))}
        const["vecs"] = m.put("vecs", 51, [P, 32])
        hd = nc.dram_tensor("expert_act", (P, KEYS, T), F).ap()
        gd = nc.dram_tensor("expert_gate", (T // 32, P, KEYS * 32), F).ap()
        score = mix_program(nc, sem, psum, m, a, acc, sT, const)
        up_program(nc, sem, psum, m, a, sT, const, score, hd, gd)
        down_program(nc, sem, psum, m, a, acc, const, hd, gd, out)


_INS = ["x", "norm_mix", "w_in", "conv_w", "conv_b", "w_branch_a", "w_branch_b", "w_out", "norm_ffn", "w_q",
        "sub_keys", "expert_u", "expert_v", "final_norm"]


def kernel(**inputs):
    import concourse.bacc as _bacc
    from concourse.bass_utils import run_bass_kernel_spmd as _run

    nc = _bacc.Bacc("TRN2", target_bir_lowering=False, num_devices=1)
    arrays, a = {}, {}
    for name in _INS:
        x = np.ascontiguousarray(inputs[name])
        arrays[f"in_{name}"] = x
        a[name] = nc.dram_tensor(f"in_{name}", x.shape, mybir.dt.from_np(x.dtype), kind="ExternalInput").ap()
    out = nc.dram_tensor("out_0", (1, T, D), F, kind="ExternalOutput").ap()
    layer(nc, a, out)
    r = _run(nc, [arrays], core_ids=[0])
    return r.results[0]["out_0"]
```

```python
from contextlib import ExitStack

import numpy as np
import concourse.bass as bass
from concourse import mybir

F = mybir.dt.float32
R = mybir.dt.float32r
U32 = mybir.dt.uint32
ALU = mybir.AluOpType
ACT = mybir.ActivationFunctionType
X = mybir.AxisListType.X
ds = bass.ds

P = 128
T = 512
D = 1024
NB = T // P
C = D // P
SBW = 512
CW = 512
HEADS = 8
PAIRS = HEADS // 2
HD = 64
CT = CW // P
KEYS = 128
LISTS = 16
TOPK = 16
EPS = 1e-6
NEG = -3.0e38
FAR = -1.0e30
KB = 1024
PRIMED = 1

Q0, K0, V0 = 0, SBW, 2 * SBW
CB0, CC0, CU0 = 3 * SBW, 3 * SBW + CW, 3 * SBW + 2 * CW
GA0 = 3 * SBW + 3 * CW
GB0 = GA0 + D

OFF = {0: (512, 384), 2: (896, 128), 1: (1024, 256)}
ZW = 1280


class Map:

    def __init__(self, nc, base):
        self.nc, self.base = nc, base

    def put(self, name, kb, shape, dt=F):
        return self.nc.alloc_sbuf_tensor_at(name, shape, dt, offset=self.base + int(kb * KB))


def mix_program(nc, sem, psum, m, a, acc, sT, const, u_raw, u_in, u_view):
    ident, iota, tri, ones, causal, gap, vecs = (const[k] for k in (
        "ident", "iota", "tri", "ones", "causal", "gap", "vecs"))
    xh, xl = sT
    score = m.put("score", 52, [P, NB, LISTS, KEYS])
    ath = m.put("ath", 52, [P, PAIRS, T], R)
    atl = m.put("atl", 60, [P, PAIRS, T], R)
    cvh = m.put("cvh", 68, [P, CT, T], R)
    cvl = m.put("cvl", 76, [P, CT, T], R)
    mgh = m.put("mgh", 84, [P, C, T], R)
    mgl = m.put("mgl", 100, [P, C, T], R)
    xn = m.put("xn", 84, [P, NB, D])
    raw = [m.put(f"raw{i}", 116 + 4 * i, [P, C, P]) for i in range(3)]
    wh = [m.put(f"wh{i}", 128 + 4 * i, [P, C, P], R) for i in range(3)]
    wl = [m.put(f"wl{i}", 140 + 4 * i, [P, C, P], R) for i in range(3)]
    z = m.put("z", 152, [P, 2, ZW])
    sp = m.put("sp", 162, [P, 2, ZW])
    qT = m.put("qT", 172, [P, T])
    kT = m.put("kT", 174, [P, T])
    vT = m.put("vT", 176, [P, T])
    v = m.put("v", 178, [P, NB, P])
    cb = m.put("cb", 180, [P, T])
    cc = m.put("cc", 182, [P, T])
    cz = m.put("cz", 184, [P, 2 + T])
    cy = m.put("cy", 187, [P, T])
    ga = m.put("ga", 189, [P, T])
    gb = m.put("gb", 191, [P, T])
    ot = [m.put(f"ot{i}", 193 + 2 * i, [P, T]) for i in range(2)]
    keyT = m.put("keyT", 152, [P, LISTS, KEYS])
    key = m.put("key", 160, [P, LISTS, P])
    rows = m.put("rows", 197, [32, P])
    zeros = m.put("zeros", 199, [P, P])
    count = m.put("count", 199.5, [P, P], U32)
    st = m.put("st", 198, [P, 4, NB])
    ss, var, rs, tmp = (st[:, i, :] for i in range(4))

    pj = psum[0:3]
    zt = psum[3:6]
    av = psum[6]
    tp = psum[7]

    S = {n: sem(n) for n in (
        "rows_in key_in sq_done var_ready root_ready xn_ready vec_T vec_in xT_full xT_hi xT_lo "
        "vT_full v_ready z_full z_copied abs_done soft_done sp_ready t_full "
        "t_used arg_ready att_ready av_full av_hi av_lo cv_y cv_hi cv_lo "
        "mg_sum mg_hi mg_lo oT_full x_added "
        "key_T key_ready s_full s_out consts vchain vmax conv wcol made raw_b").split()}
    raw_in = [sem(f"raw_in{i}") for i in range(3)]
    w_hi = [sem(f"w_hi{i}") for i in range(3)]
    w_lo = [sem(f"w_lo{i}") for i in range(3)]
    tile_done = [sem(f"tile_done{i}") for i in range(3)]
    taken = [sem(f"taken{i}") for i in range(3)]

    x_in = [sem(f"x_in{b}") for b in range(NB)]
    nb_ring = [psum[3], psum[5], psum[6], psum[7]]
    w_in = a["w_in"][0].rearrange("(c p) f -> p c f", p=P)
    w_q = a["w_q"][0].rearrange("(c p) f -> p c f", p=P)
    w_o = a["w_out"][0].rearrange("(c p) f -> p c f", p=P)
    w_a = a["w_branch_a"][0].rearrange("(c p) f -> p c f", p=P)
    w_b = a["w_branch_b"][0].rearrange("(c p) f -> p c f", p=P)
    L4 = 16

    with nc.Block() as block:
        @block.sync
        def _(sp_):
            for free in (*w_lo, *(S[n] for n in ("t_used", "av_lo", "x_added", "s_out", "oT_full", "s_full"))):
                sp_.sem_inc(free, PRIMED)
            for b in range(NB):
                sp_.dma_start(acc[:, b, :], a["x"][0, b * P:(b + 1) * P, :]).then_inc(x_in[b], 16)
            for r0, n, src in ((0, C, a["norm_mix"][0].rearrange("(c p) -> c p", p=P)),
                               (8, C, a["norm_ffn"][0].rearrange("(c p) -> c p", p=P)),
                               (16, 12, a["conv_w"][0].rearrange("k o (t p) -> (k o t) p", p=P)),
                               (28, CT, a["conv_b"][0].rearrange("(t p) -> t p", p=P))):
                sp_.dma_start(rows[r0:r0 + n, :], src).then_inc(S["rows_in"], 16)

            def load(slot, r, src):
                sp_.wait_ge(S["rows_in"], 64)
                sp_.wait_ge(w_lo[slot], r + PRIMED)
                n = src.shape[1]
                sp_.dma_start(raw[slot][:, 0:n, :], src).then_inc(raw_in[slot], 16)

            with sp_.Fori(0, PAIRS) as p:
                for slot, f0 in enumerate((Q0, K0, V0)):
                    load(slot, p * 2, w_in[:, :, ds(p * P + f0, P)])
                for slot, f0 in enumerate((CB0, CC0, CU0)):
                    load(slot, p * 2 + 1, w_in[:, :, ds(p * P + f0, P)])
            with sp_.Fori(0, C) as c:
                load(0, c + 8, w_in[:, :, ds(c * P + GA0, P)])
                load(1, c + 8, w_in[:, :, ds(c * P + GB0, P)])
                load(2, c + 8, w_a[:, :, ds(c * P, P)])
                sp_.dma_start(raw[2][:, 4:8, :], w_b[:, :, ds(c * P, P)]).then_inc(S["raw_b"], 16)
            with sp_.Fori(0, C // 2) as i:
                for slot in range(2):
                    load(slot, i + L4, w_o[:, :, ds(i * 2 * P + slot * P, P)])
            sp_.wait_ge(S["av_hi"], PAIRS)
            sp_.dma_start(key[:], a["sub_keys"][0].rearrange("h q k c -> k (h q) c")).then_inc(S["key_in"], 16)
            with sp_.Fori(0, LISTS // 2) as i:
                for slot in range(2):
                    load(slot, i + (L4 + C // 2), w_q[:, :, ds(i * 2 * P + slot * P, P)])
            sp_.wait_ge(S["x_added"], C + PRIMED)
            for i in range(2):
                sp_.dma_start(u_raw[i][:].unsqueeze(1), u_view[:, i:i + 1, :]).then_inc(u_in[i], 16)

        @block.gpsimd
        def _(pool):
            nc.gpsimd.memset(ones[:], 1.0)
            nc.gpsimd.memset(zeros[:], 0.0)
            nc.gpsimd.iota(count[:], pattern=[[1, P]], base=0, channel_multiplier=0).then_inc(S["made"], 1)
            pool.wait_ge(S["made"], 1)
            nc.gpsimd.tensor_copy(iota[:], count[:])
            for out_, in_, op, fill, step, per in (
                    (ident, zeros, ALU.not_equal, 1.0, -1, 1),
                    (tri, ones, ALU.is_ge, 0.0, -1, 1),
                    (causal, ones, ALU.is_gt, 0.0, 1, -1),
                    (gap, zeros, ALU.is_gt, FAR, 1, -1)):
                last = nc.gpsimd.affine_select(out=out_[:], in_=in_[:], compare_op=op, fill=fill, base=0,
                                               pattern=[[step, P]], channel_multiplier=per)
            last.then_inc(S["consts"], 1)

            def split(slot, r):
                pool.wait_ge(w_hi[slot], r + 1)
                nc.gpsimd.tensor_tensor(wl[slot][:], raw[slot][:], wh[slot][:].bitcast(F),
                                        ALU.subtract).then_inc(w_lo[slot], 1)

            with pool.Fori(0, PAIRS + CT) as r:
                for slot in range(3):
                    split(slot, r)
            with pool.Fori(0, C) as c:
                for slot in range(3):
                    split(slot, c + (PAIRS + CT))
            with pool.Fori(L4, L4 + 12) as r:
                for slot in range(2):
                    split(slot, r)

        @block.tensor
        def _(pe):
            def three_pass(out, slot, hi, lo, chunks, w0=0):
                for i in range(chunks):
                    for n, (w, x) in enumerate(((wh, hi), (wh, lo), (wl, hi))):
                        last = nc.tensor.matmul(out, w[slot][:, w0 + i, :], x[:, i, :],
                                                start=(i == 0 and n == 0), stop=(i == chunks - 1 and n == 2))
                return last

            def project(slot, r, hi, lo):
                pe.wait_ge(w_lo[slot], r + 1 + PRIMED)
                pe.wait_ge(taken[slot], r)
                three_pass(pj[slot][:], slot, hi, lo, C).then_inc(tile_done[slot], 1)

            def norm_transposes(first, n0):
                pe.wait_ge(S["xn_ready"], n0)
                for c in range(C):
                    if c >= len(nb_ring):
                        pe.wait_ge(S["xT_lo"], first + c - len(nb_ring) + 1)
                    for b in range(NB):
                        last = nc.tensor.transpose(nb_ring[c % 4][:, b * P:(b + 1) * P],
                                                   xn[:, b, c * P:(c + 1) * P], ident[:])
                    last.then_inc(S["xT_full"], 1)

            def scores(p):
                pe.wait_ge(taken[1], p * 2 + 1)
                for e in range(2):
                    h = slice(e * HD, (e + 1) * HD)
                    pe.wait_ge(S["t_used"], p * 2 + PRIMED)
                    if e:
                        pe.wait_ge(S["z_copied"], p * 2 + 1)
                    for b in range(NB):
                        nc.tensor.matmul(zt[0][:, b * P:(b + 1) * P], kT[h, b * P:(b + 1) * P],
                                         qT[h, b * P:(b + 1) * P], start=True, stop=True)
                    for kb, (o, n) in OFF.items():
                        last = nc.tensor.matmul(zt[o // T][:, o % T:o % T + n], kT[h, kb * P:(kb + 1) * P],
                                                qT[h, (kb + 1) * P:], start=True, stop=True)
                    last.then_inc(S["z_full"], 1)

            def sums(p):
                for e in range(2):
                    pe.wait_ge(S["sp_ready"], p * 2 + e + 1)
                    pe.wait_ge(S["z_copied"], p * 2 + 2)
                    pe.wait_ge(S["t_used"], p * 2 + e + PRIMED)
                    for b in range(NB):
                        nc.tensor.matmul(zt[0][:, b * P:(b + 1) * P], tri[:], sp[:, e, b * P:(b + 1) * P],
                                         start=True, stop=True)
                    for kb, (o, n) in OFF.items():
                        bank, o0 = zt[o // T], o % T
                        parts = [(tri, o, n, o0)]
                        for jb in range(kb + 1, NB):
                            at = o0 + (jb - kb - 1) * P
                            parts.append((ones, jb * P, P, at))
                            if jb < NB - 1:
                                parts.append((ones, OFF[jb][0], OFF[jb][1], at + P))
                        for n_, (w, src, width, at) in enumerate(parts):
                            last = nc.tensor.matmul(bank[:, at:at + width], w[:], sp[:, e, src:src + width],
                                                    start=(n_ == 0), stop=(n_ == len(parts) - 1))
                    last.then_inc(S["t_full"], 1)

            def outputs(p):
                pe.wait_ge(S["av_lo"], p + PRIMED)
                pe.wait_ge(S["v_ready"], p + 1)
                for e in range(2):
                    h = slice(e * HD, (e + 1) * HD)
                    pe.wait_ge(S["att_ready"], p * 2 + e + 1)
                    parts = [(kb, *OFF[kb], (kb + 1) * P) for kb in (0, 1, 2)] + [(b, b * P, P, b * P) for b in range(NB)]
                    for n_, (kb, src, width, at) in enumerate(parts):
                        last = nc.tensor.matmul(av[h, at:at + width], v[:, kb, h], z[:, e, src:src + width],
                                                start=(n_ == 0), stop=(n_ == len(parts) - 1))
                last.then_inc(S["av_full"], 1)

            def transpose_v(p):
                pe.wait_ge(taken[2], p * 2 + 1)
                for b in range(NB):
                    last = nc.tensor.transpose(tp[:, b * P:(b + 1) * P], vT[:, b * P:(b + 1) * P], ident[:])
                last.then_inc(S["vT_full"], 1)

            pe.wait_ge(S["consts"], 1)
            pe.wait_ge(S["rows_in"], 64)
            nc.tensor.transpose(pj[0][:, 0:32], rows[:, :], ident[0:32, 0:32]).then_inc(S["vec_T"], 1)
            norm_transposes(0, NB)
            pe.wait_ge(S["xT_lo"], C)
            pe.wait_ge(S["vec_in"], 1)

            def pair(p, r, before=None):
                project(0, r, xh, xl)
                project(1, r, xh, xl)
                if before is not None:
                    outputs(before)
                project(2, r, xh, xl)
                transpose_v(p)
                scores(p)
                for slot in range(3):
                    project(slot, r + 1, xh, xl)
                sums(p)

            pair(0, 0)
            with pe.Fori(1, PAIRS) as p:
                pair(p, p * 2, before=p - 1)

            def gated(r, before=None):
                project(0, r, xh, xl)
                project(1, r, xh, xl)
                if before is not None:
                    outputs(before)
                pe.wait_ge(S["av_lo"], PAIRS + PRIMED)
                pe.wait_ge(S["cv_lo"], CT)
                pe.wait_ge(w_lo[2], r + 1 + PRIMED)
                pe.wait_ge(taken[2], r)
                three_pass(pj[2][:], 2, ath, atl, 4)
                three_pass(zt[0][:], 2, cvh, cvl, 4, w0=4).then_inc(tile_done[2], 1)

            gated(PAIRS * 2, before=PAIRS - 1)
            with pe.Fori(PAIRS * 2 + 1, L4) as r:
                gated(r)
            pe.wait_ge(S["mg_lo"], C)

            def transpose_out(slot, i):
                pe.wait_ge(taken[slot], i + (L4 + 1))
                pe.wait_ge(S["x_added"], i * 2 + slot + PRIMED)
                for b in range(NB):
                    last = nc.tensor.transpose(tp[:, b * P:(b + 1) * P], ot[slot][:, b * P:(b + 1) * P], ident[:])
                last.then_inc(S["oT_full"], 1)

            project(0, L4, mgh, mgl)
            with pe.Fori(0, C // 2 - 1) as i:
                project(1, i + L4, mgh, mgl)
                transpose_out(0, i)
                project(0, i + (L4 + 1), mgh, mgl)
                transpose_out(1, i)
            project(1, L4 + C // 2 - 1, mgh, mgl)
            transpose_out(0, C // 2 - 1)
            transpose_out(1, C // 2 - 1)
            pe.wait_ge(S["key_in"], 16)
            for g in range(LISTS // 4):
                pe.wait_ge(S["key_ready"], g)
                for q in range(4):
                    last = nc.tensor.transpose(zt[1][:, q * P:(q + 1) * P], key[:, 4 * g + q, :], ident[:])
                last.then_inc(S["key_T"], 1)
            norm_transposes(C, 2 * NB)
            pe.wait_ge(S["xT_lo"], 2 * C)
            pe.wait_ge(S["key_ready"], LISTS // 4)

            def score_list(slot, i):
                pe.wait_ge(taken[slot], i + (L4 + C // 2 + 1))
                pe.wait_ge(S["s_out"], i * 2 + PRIMED)
                at = slice(i * 2 + slot, i * 2 + slot + 1) if isinstance(i, int) else ds(i * 2 + slot, 1)
                for b in range(NB):
                    last = nc.tensor.matmul(zt[slot][:, b * P:(b + 1) * P], ot[slot][:, b * P:(b + 1) * P],
                                            keyT[:, at, :], start=True, stop=True)
                last.then_inc(S["s_full"], 1)

            L5 = L4 + C // 2
            project(0, L5, xh, xl)
            with pe.Fori(0, LISTS // 2 - 1) as i:
                project(1, i + L5, xh, xl)
                score_list(0, i)
                project(0, i + (L5 + 1), xh, xl)
                score_list(1, i)
            project(1, L5 + LISTS // 2 - 1, xh, xl)
            score_list(0, LISTS // 2 - 1)
            score_list(1, LISTS // 2 - 1)

        @block.scalar
        def _(act):
            def squares(first):
                for b in range(NB):
                    if first == 0:
                        act.wait_ge(x_in[b], 16)
                    nc.scalar.activation(xn[:, b, :], acc[:, b, :], ACT.Square,
                                         accum_out=ss[:, b:b + 1]).then_inc(S["sq_done"], 1)
                act.wait_ge(S["var_ready"], first + 1)
                nc.scalar.activation(rs, var, ACT.Sqrt).then_inc(S["root_ready"], 1)

            def norm_hi(first, gain):
                for c in range(C):
                    act.wait_ge(S["xT_full"], first + c + 1)
                    nc.scalar.activation(xh[:, c, :], nb_ring[c % 4][:], ACT.Copy,
                                         scale=vecs[:, gain + c:gain + c + 1]).then_inc(S["xT_hi"], 1)

            def copy_scores(p):
                for e in range(2):
                    act.wait_ge(S["z_full"], p * 2 + e + 1)
                    for b, n in enumerate((T, T, ZW - 2 * T)):
                        last = nc.scalar.activation(z[:, e, b * T:b * T + n], zt[b][:, 0:n], ACT.Copy)
                    last.then_inc(S["z_copied"], 1)

            def softplus(p):
                act.wait_ge(S["abs_done"], p + 1)
                nc.scalar.activation(sp[:], sp[:], ACT.Exp, scale=-1.0).then_inc(S["soft_done"], 1)
                act.wait_ge(S["soft_done"], p * 2 + 1)
                nc.scalar.activation(sp[:], sp[:], ACT.Ln, bias=1.0).then_inc(S["soft_done"], 1)

            def exps(p):
                for e in range(2):
                    act.wait_ge(S["arg_ready"], p * 2 + e + 1)
                    nc.scalar.activation(z[:, e, :], z[:, e, :], ACT.Exp).then_inc(S["att_ready"], 1)

            def attention_hi(p):
                act.wait_ge(S["av_full"], p + 1)
                nc.scalar.activation(ath[:, ds(p, 1), :] if not isinstance(p, int) else ath[:, p:p + 1, :],
                                     av[:], ACT.Copy).then_inc(S["av_hi"], 1)

            def take(slot, r, out, func=ACT.Copy, scale=1.0):
                act.wait_ge(tile_done[slot], r + 1)
                nc.scalar.activation(out, pj[slot][:], func, scale=scale).then_inc(taken[slot], 1)

            def high(slot, r):
                act.wait_ge(raw_in[slot], r * 16 + 16)
                act.wait_ge(tile_done[slot], r)
                nc.scalar.activation(wh[slot][:], raw[slot][:], ACT.Copy).then_inc(w_hi[slot], 1)

            def both_highs(c):
                act.wait_ge(S["raw_b"], c * 16 + 16)
                high(2, c + (PAIRS + CT))

            squares(0)
            high(0, 0)
            high(1, 0)
            nc.scalar.preload_act_table_set("natural_log_exp_and_others")
            norm_hi(0, 0)

            def conv_hi(t):
                at = slice(t, t + 1) if isinstance(t, int) else ds(t, 1)
                act.wait_ge(S["cv_y"], t + 1)
                nc.scalar.activation(cvh[:, at, :], cy[:].unsqueeze(1), ACT.Copy).then_inc(S["cv_hi"], 1)

            def pair(p, r, before=None):
                high(2, r)
                take(0, r, qT[:], scale=HD ** -0.5)
                high(0, r + 1)
                if before is not None:
                    exps(before)
                take(1, r, kT[:])
                high(1, r + 1)
                if before is not None:
                    attention_hi(before)
                take(2, r, vT[:])
                high(2, r + 1)
                copy_scores(p)
                take(0, r + 1, cb[:])
                high(0, r + 2)
                softplus(p)
                take(1, r + 1, cc[:])
                high(1, r + 2)
                conv_hi(p)

            pair(0, 0)
            with act.Fori(1, PAIRS) as p:
                pair(p, p * 2, before=p - 1)
            R0 = PAIRS * 2

            def gated(r, c, ahead, before=None):
                both_highs(c)
                take(0, r, ga[:], ACT.Sigmoid)
                high(0, r + 1)
                if before is not None:
                    exps(before)
                take(1, r, gb[:], ACT.Sigmoid)
                high(1, r + 1)
                if before is not None:
                    attention_hi(before)
                at = slice(c, c + 1) if isinstance(c, int) else ds(c, 1)
                act.wait_ge(S["mg_sum"], c + 1)
                nc.scalar.activation(mgh[:, at, :], ga[:].unsqueeze(1), ACT.Copy).then_inc(S["mg_hi"], 1)
                act.wait_ge(S["mg_lo"], c + 1)

            gated(R0, 0, True, before=PAIRS - 1)
            nc.scalar.preload_act_table_set("sigmoid_and_others")
            with act.Fori(R0 + 1, L4) as r:
                gated(r, r - R0, True)
            with act.Fori(0, C // 2) as i:
                for slot in range(2):
                    act.wait_ge(S["oT_full"], i * 2 + PRIMED)
                    take(slot, i + L4, ot[slot][:])
                    high(slot, i + (L4 + 1))
            for g in range(LISTS // 4):
                act.wait_ge(S["key_T"], g + 1)
                nc.scalar.activation(keyT[:, 4 * g:4 * g + 4, :], zt[1][:], ACT.Copy).then_inc(S["key_ready"], 1)
            act.wait_ge(S["x_added"], C + PRIMED)
            squares(1)
            norm_hi(C, C)

            def take_query(i, slot):
                act.wait_ge(S["s_full"], i * 2 + PRIMED)
                take(slot, i + (L4 + C // 2), ot[slot][:])

            with act.Fori(0, LISTS // 2 - 1) as i:
                for slot in range(2):
                    take_query(i, slot)
                    high(slot, i + (L4 + C // 2 + 1))
            for slot in range(2):
                take_query(LISTS // 2 - 1, slot)

        @block.vector
        def _(dve):
            done = [0]

            def chain(ins):
                done[0] += 1
                ins.then_inc(S["vchain"], 1)
                dve.wait_ge(S["vchain"], done[0])

            def normed(first):
                dve.wait_ge(S["sq_done"], (first + 1) * NB)
                nc.vector.tensor_scalar(var, ss, 1.0 / D, EPS, ALU.mult, ALU.add).then_inc(S["var_ready"], 1)
                dve.wait_ge(S["root_ready"], first + 1)
                chain(nc.vector.reciprocal(rs, rs))
                chain(nc.vector.tensor_tensor(tmp, rs, rs, ALU.mult))
                chain(nc.vector.tensor_tensor(tmp, tmp, var, ALU.mult))
                chain(nc.vector.tensor_scalar(tmp, tmp, -0.5, 1.5, ALU.mult, ALU.add))
                chain(nc.vector.tensor_tensor(rs, rs, tmp, ALU.mult))
                for b in range(NB):
                    nc.vector.tensor_scalar(xn[:, b, :], acc[:, b, :], rs[:, b:b + 1], None,
                                            ALU.mult).then_inc(S["xn_ready"], 1)

            def norm_lo(first, gain):
                for c in range(C):
                    dve.wait_ge(S["xT_hi"], first + c + 1)
                    nc.vector.scalar_tensor_tensor(xl[:, c, :], nb_ring[c % 4][:], vecs[:, gain + c:gain + c + 1],
                                                   xh[:, c, :].bitcast(F), ALU.mult,
                                                   ALU.subtract).then_inc(S["xT_lo"], 1)

            chain(nc.vector.memset(cz[:, 0:2], 0.0))
            dve.wait_ge(S["vec_T"], 1)
            nc.vector.tensor_copy(vecs[:], pj[0][:, 0:32]).then_inc(S["vec_in"], 1)
            dve.wait_ge(S["vec_in"], 1)
            normed(0)
            norm_lo(0, 0)

            def take_v(p):
                dve.wait_ge(S["vT_full"], p + 1)
                nc.vector.tensor_copy(v[:], tp[:].rearrange("p (b f) -> p b f", b=NB)).then_inc(S["v_ready"], 1)

            diag = lambda x, e: x[:, e, 0:T].rearrange("p (b q) -> p b q", b=NB)
            wide = lambda x: x[:].unsqueeze(1).broadcast_to([P, NB, P])

            def magnitudes(p):
                dve.wait_ge(S["z_copied"], p * 2 + 2)
                nc.vector.scalar_tensor_tensor(sp[:], z[:], -1.0, z[:], ALU.mult, ALU.max).then_inc(S["abs_done"], 1)

            def soft(p):
                for e in range(2):
                    dve.wait_ge(S["soft_done"], p * 2 + 2)
                    nc.vector.scalar_tensor_tensor(sp[:, e, :], z[:, e, :], 0.0, sp[:, e, :], ALU.max,
                                                   ALU.add).then_inc(S["vmax"], 1)
                    dve.wait_ge(S["vmax"], p * 2 + e + 1)
                    nc.vector.tensor_tensor(diag(sp, e), diag(sp, e), wide(causal), ALU.mult).then_inc(S["sp_ready"], 1)

            def arguments(p):
                for e in range(2):
                    dve.wait_ge(S["t_full"], p * 2 + e + 1)
                    for b, n in enumerate((T, T, ZW - 2 * T)):
                        last = nc.vector.tensor_tensor(z[:, e, b * T:b * T + n], z[:, e, b * T:b * T + n],
                                                       zt[b][:, 0:n], ALU.subtract)
                    last.then_inc(S["t_used"], 1)
                    dve.wait_ge(S["t_used"], p * 2 + e + 1 + PRIMED)
                    chained = nc.vector.scalar_tensor_tensor(diag(z, e), diag(z, e), 0.0, wide(gap), ALU.min,
                                                             ALU.add)
                    chained.then_inc(S["arg_ready"], 1)

            def attention_lo(p):
                dve.wait_ge(S["av_hi"], p + 1)
                at = slice(p, p + 1) if isinstance(p, int) else ds(p, 1)
                nc.vector.tensor_tensor(atl[:, at, :], av[:].unsqueeze(1), ath[:, at, :].bitcast(F),
                                        ALU.subtract).then_inc(S["av_lo"], 1)

            wcol = m.put("wcol", 198.5, [P, 4])

            def convolve(t):
                def step(n, ins):
                    ins.then_inc(S["conv"], 1)
                    dve.wait_ge(S["conv"], t * 3 + n)
                cols = vecs[:, 16:32].rearrange("p (k t) -> p k t", k=4)
                at = slice(t, t + 1) if isinstance(t, int) else ds(t, 1)
                nc.vector.tensor_copy(wcol[:].unsqueeze(2), cols[:, :, at]).then_inc(S["wcol"], 1)
                dve.wait_ge(S["wcol"], t + 1)
                dve.wait_ge(taken[1], t * 2 + 2)
                dve.wait_ge(tile_done[2], t * 2 + 2)
                nc.vector.tensor_tensor(cz[:, 2:2 + T], pj[2][:], cc[:], ALU.mult).then_inc(taken[2], 1)
                dve.wait_ge(taken[2], t * 2 + 2)
                step(1, nc.vector.tensor_scalar(cy[:], cz[:, 2:2 + T], wcol[:, 2:3], wcol[:, 3:4], ALU.mult, ALU.add))
                step(2, nc.vector.scalar_tensor_tensor(cy[:], cz[:, 1:1 + T], wcol[:, 1:2], cy[:], ALU.mult, ALU.add))
                step(3, nc.vector.scalar_tensor_tensor(cy[:], cz[:, 0:T], wcol[:, 0:1], cy[:], ALU.mult, ALU.add))
                nc.vector.tensor_tensor(cy[:], cy[:], cb[:], ALU.mult).then_inc(S["cv_y"], 1)
                dve.wait_ge(S["cv_hi"], t + 1)
                nc.vector.tensor_tensor(cvl[:, at, :], cy[:].unsqueeze(1), cvh[:, at, :].bitcast(F),
                                        ALU.subtract).then_inc(S["cv_lo"], 1)

            def pair(p, before=None):
                if before is not None:
                    attention_lo(before)
                take_v(p)
                magnitudes(p)
                soft(p)
                convolve(p)
                arguments(p)

            pair(0)
            with dve.Fori(1, PAIRS) as p:
                pair(p, before=p - 1)
            attention_lo(PAIRS - 1)

            with dve.Fori(0, C) as c:
                dve.wait_ge(taken[1], c + (PAIRS + CT + 1))
                dve.wait_ge(tile_done[2], c + (PAIRS + CT + 1))
                nc.vector.tensor_tensor(gb[:], gb[:], zt[0][:], ALU.mult)
                nc.vector.tensor_tensor(ga[:], ga[:], pj[2][:], ALU.mult).then_inc(taken[2], 1)
                dve.wait_ge(taken[2], c + (PAIRS + CT + 1))
                nc.vector.tensor_tensor(ga[:], ga[:], gb[:], ALU.add).then_inc(S["mg_sum"], 1)
                dve.wait_ge(S["mg_hi"], c + 1)
                nc.vector.tensor_tensor(mgl[:, ds(c, 1), :], ga[:].unsqueeze(1), mgh[:, ds(c, 1), :].bitcast(F),
                                        ALU.subtract).then_inc(S["mg_lo"], 1)

            with dve.Fori(0, C) as c:
                dve.wait_ge(S["oT_full"], c + 1 + PRIMED)
                part = acc[:, :, ds(c * P, P)]
                nc.vector.tensor_tensor(part, part, tp[:].rearrange("p (b f) -> p b f", b=NB),
                                        ALU.add).then_inc(S["x_added"], 1)
            normed(1)
            norm_lo(C, C)
            with dve.Fori(0, LISTS // 2) as i:
                for slot in range(2):
                    dve.wait_ge(S["s_full"], i * 2 + slot + 1 + PRIMED)
                    nc.vector.tensor_copy(score[:, :, ds(i * 2 + slot, 1), :],
                                          zt[slot][:].rearrange("p (b o k) -> p b o k", b=NB, o=1)).then_inc(S["s_out"], 1)
    return score


def up_program(nc, sem, psum, m, a, sT, const, score, hd, gd, raw, u_in, u_view, first_loads):
    ident, iota = const["ident"], const["iota"]
    xh, xl = sT
    uh = [m.put(f"uh{i}", 84 + 4 * i, [P, C, P], R) for i in range(2)]
    ul = [m.put(f"ul{i}", 92 + 4 * i, [P, C, P], R) for i in range(2)]
    hb = [m.put(f"hb{i}", 108 + 2 * i, [P, T]) for i in range(2)]
    grid = [m.put(f"grid{i}", 112 + 16 * i, [P, KEYS, 32]) for i in range(2)]
    lists = m.put("lists", 144, [P, 2, KEYS])
    left = m.put("left", 145, [P, 2, KEYS])
    top = m.put("top", 149.5, [P, 2, TOPK])
    cand = m.put("cand", 146, [P, TOPK, TOPK])
    cleft = m.put("cleft", 147, [P, TOPK, TOPK])
    best = m.put("best", 148, [P, TOPK])
    picks = m.put("picks", 148.5, [P, 4, TOPK], U32)
    pos = m.put("pos", 149, [P, TOPK], U32)
    best_all = m.put("best_all", 150, [P, NB * HEADS, TOPK])
    picks_all = m.put("picks_all", 152, [P, NB * HEADS, 4, TOPK])
    sel = m.put("sel", 160, [P, 3, HEADS * TOPK])
    peak = m.put("peak", 162, [P, 2, HEADS])
    selT = m.put("selT", 163, [P, 3, T])
    eq = [m.put(f"eq{i}", 170 + 8 * i, [P, HEADS * TOPK, TOPK]) for i in range(2)]
    hot = [m.put(f"hot{i}", 170 + 12 * i, [P, 8, 3, KEYS], R) for i in range(2)]
    gate_hi = m.put("gate_hi", 194, [P, T], R)
    gate_lo = m.put("gate_lo", 196, [P, T])

    utp = [psum[0:2], psum[2:4]]
    zb = psum[4:6]
    gp = psum[6:8]

    ut_full, ut_hi, ut_lo, u_mm, h_done, h_out, hot_ready, g_full, g_out = (
        [sem(f"{n}{i}") for i in range(2)] for n in (
            "ut_full", "ut_hi", "ut_lo", "u_mm", "h_done", "h_out", "hot_ready", "g_full", "g_out"))
    S = {n: sem(n) for n in ("pick picked sel_in exp_in exp_out sel_ready selT_full selT_in "
                             "l2_chain g_evac gate_split").split()}
    eq_hot, eq_key = [sem(f"eq_hot{i}") for i in range(2)], [sem(f"eq_key{i}") for i in range(2)]
    hv = hd.rearrange("i (r s) t -> i r s t", s=2)
    uv = u_view.rearrange("i (r s) d -> i r s d", s=2)

    N1, N2, N3, N4 = 24, NB, 32, 4
    assert N1 + N2 + N3 + N4 == KEYS // 2

    with nc.Block() as block:
        @block.sync
        def _(sp_):
            for free in (*ut_full, *ut_lo, *h_done, *u_mm, *g_full, *(S[n] for n in ("selT_in", "g_evac", "selT_full"))):
                sp_.sem_inc(free, PRIMED)
            for free in (*h_out, *g_out):
                sp_.sem_inc(free, PRIMED * 16)
            def load(r):
                for s in range(2):
                    sp_.wait_ge(ut_full[s], r + PRIMED)
                    sp_.dma_start(raw[s][:].unsqueeze(1), uv[:, ds(r, 1), s, :]).then_inc(u_in[s], 16)

            with sp_.Fori(1, KEYS // 2 - N4) as r:
                load(r)
            sp_.wait_ge(S["picked"], NB * HEADS)
            for s in range(2):
                first_loads(sp_, s, 0)
            with sp_.Fori(KEYS // 2 - N4, KEYS // 2) as r:
                load(r)
            sp_.wait_ge(S["g_evac"], N3 * 2 + PRIMED)
            for s in range(2):
                sp_.wait_ge(g_out[s], (N3 // 4 + PRIMED) * 16)
                sp_.wait_ge(h_out[s], (4 + PRIMED) * 16)
            for s in range(2):
                first_loads(sp_, s, 1)

        @block.tensor
        def _(pe):
            def transposes(s, r):
                pe.wait_ge(u_in[s], r * 16 + 16)
                pe.wait_ge(ut_lo[s], r + PRIMED)
                for c in range(C):
                    last = nc.tensor.transpose(utp[s][c // 4][:, c % 4 * P:(c % 4 + 1) * P],
                                               raw[s][:, c * P:(c + 1) * P], ident[:])
                last.then_inc(ut_full[s], 1)

            def products(s, r):
                pe.wait_ge(ut_lo[s], r + 1 + PRIMED)
                pe.wait_ge(h_done[s], r + PRIMED)
                for c in range(C):
                    for n, (w, x) in enumerate(((uh, xh), (uh, xl), (ul, xh))):
                        last = nc.tensor.matmul(zb[s][:], w[s][:, c, :], x[:, c, :],
                                                start=(c == 0 and n == 0), stop=(c == C - 1 and n == 2))
                last.then_inc(u_mm[s], 1)

            def step(s, r, ahead=True):
                if ahead:
                    transposes(1 - s, r + s)
                products(s, r)

            def spread(s, r, k):
                pe.wait_ge(hot_ready[s], r + 1)
                pe.wait_ge(S["g_evac"], k + PRIMED)
                for n in range(8):
                    for part in (1, 2):
                        last = nc.tensor.matmul(gp[n // 4][:, n % 4 * P:(n % 4 + 1) * P], hot[s][:, n, 0, :],
                                                hot[s][:, n, part, :], start=(part == 1), stop=(part == 2))
                last.then_inc(g_full[s], 1)

            transposes(0, 0)
            with pe.Fori(0, N1) as r:
                for s in range(2):
                    step(s, r)
            with pe.Fori(0, N2) as b:
                for s in range(2):
                    step(s, b + N1)
                pe.wait_ge(S["sel_ready"], b * 2 + 2)
                pe.wait_ge(S["selT_in"], b + PRIMED)
                for n in range(3):
                    last = nc.tensor.transpose(gp[0][:, n * P:(n + 1) * P], sel[:, n, :], ident[:])
                last.then_inc(S["selT_full"], 1)
            step(0, N1 + N2)
            with pe.Fori(0, N3 // 4) as q:
                for j in range(8):
                    step((j + 1) % 2, q * 4 + (N1 + N2 + (j + 1) // 2))
                    spread(j % 2, q * 4 + j // 2, q * 8 + j)
            step(1, N1 + N2 + N3)
            with pe.Fori(N1 + N2 + N3 + 1, KEYS // 2 - 1) as r:
                for s in range(2):
                    step(s, r)
            step(0, KEYS // 2 - 1)
            step(1, KEYS // 2 - 1, ahead=False)

        @block.scalar
        def _(act):
            def high(s, r):
                act.wait_ge(ut_full[s], r + 1 + PRIMED)
                act.wait_ge(u_mm[s], r + PRIMED)
                for g in range(2):
                    last = nc.scalar.activation(uh[s][:, 4 * g:4 * g + 4, :], utp[s][g][:], ACT.Copy)
                last.then_inc(ut_hi[s], 1)

            def gelu(s, r):
                act.wait_ge(u_mm[s], r + 1 + PRIMED)
                act.wait_ge(h_out[s], r * 16 + PRIMED * 16)
                nc.scalar.activation(hb[s][:], zb[s][:], ACT.Gelu).then_inc(h_done[s], 1)
                act.wait_ge(h_done[s], r + 1 + PRIMED)
                at = slice(r, r + 1) if isinstance(r, int) else ds(r, 1)
                act.dma_start(hv[:, at, s, :], hb[s][:].unsqueeze(1)).then_inc(h_out[s], 16)

            def step(s, r, ahead=True):
                if ahead:
                    high(1 - s, r + s)
                gelu(s, r)

            nc.scalar.preload_act_table_set("gelu_and_others")
            high(0, 0)
            with act.Fori(0, N1) as r:
                for s in range(2):
                    step(s, r)
            with act.Fori(0, N2) as b:
                high(1, b + N1)
                act.wait_ge(S["exp_in"], b + 1)
                nc.scalar.activation(sel[:, 2, :], sel[:, 2, :], ACT.Exp).then_inc(S["exp_out"], 1)
                gelu(0, b + N1)
                step(1, b + N1)
            nc.scalar.preload_act_table_set("gelu_and_others")
            step(0, N1 + N2)
            with act.Fori(0, N3 // 4) as q:
                for j in range(8):
                    step((j + 1) % 2, q * 4 + (N1 + N2 + (j + 1) // 2))
                    half, n0 = j // 4, j % 4 * 8
                    act.wait_ge(g_full[j % 2], q * 4 + (j // 2 + 1) + PRIMED)
                    if j % 4 == 0:
                        act.wait_ge(g_out[half], q * 16 + PRIMED * 16)
                    for g in range(2):
                        last = nc.scalar.activation(
                            grid[half][:, :, n0 + 4 * g:n0 + 4 * g + 4].rearrange("p j n -> p n j"),
                            gp[g][:].rearrange("p (n j) -> p n j", n=4), ACT.Copy)
                    last.then_inc(S["g_evac"], 1)
                    if j % 4 == 3:
                        act.wait_ge(S["g_evac"], q * 8 + j + 1 + PRIMED)
                        act.dma_start(gd[:, :, :].rearrange("b p x -> p b x")[:, ds(q * 2 + half, 1), :],
                                      grid[half][:].rearrange("p j n -> p (j n)").unsqueeze(1)).then_inc(g_out[half], 16)
            step(1, N1 + N2 + N3)
            with act.Fori(N1 + N2 + N3 + 1, KEYS // 2 - 1) as r:
                for s in range(2):
                    step(s, r)
            step(0, KEYS // 2 - 1)
            step(1, KEYS // 2 - 1, ahead=False)
            for s in range(2):
                act.wait_ge(h_out[s], KEYS // 2 * 16 + PRIMED * 16)
                act.wait_ge(g_out[s], N3 // 4 * 16 + PRIMED * 16)

        @block.gpsimd
        def _(pool):
            with pool.Fori(0, NB) as b:
                for n in range(2):
                    pool.wait_ge(eq_hot[n], b + 1)
                    view = eq[n][:].rearrange("p (h k) x -> p h k x", h=HEADS)
                    keys = picks_all[:, ds(b * HEADS, HEADS), 2 + n, :].unsqueeze(2)
                    nc.gpsimd.tensor_tensor(view, view, keys.broadcast_to([P, HEADS, TOPK, TOPK]),
                                            ALU.mult).then_inc(eq_key[n], 1)
        @block.vector
        def _(dve):
            def low(s, r):
                dve.wait_ge(ut_hi[s], r + 1)
                for g in range(2):
                    last = nc.vector.tensor_tensor(ul[s][:, 4 * g:4 * g + 4, :].rearrange("p c f -> p (c f)"), utp[s][g][:],
                                                   uh[s][:, 4 * g:4 * g + 4, :].rearrange("p c f -> p (c f)").bitcast(F), ALU.subtract)
                last.then_inc(ut_lo[s], 1)

            def pick(u):
                n = [0]

                def step(*group):
                    for ins in group:
                        n[0] += 1
                        ins.then_inc(S["pick"], 1)
                    dve.wait_ge(S["pick"], n[0])

                v = nc.vector
                flat = score[:].rearrange("p b (h q) k -> p (b h) q k", q=2)
                best8, rest8 = slice(0, 8), slice(8, 16)
                flat_c, flat_l = (t[:].rearrange("p x y -> p (x y)") for t in (cand, cleft))

                def first():
                    dve.drain()
                    dve.sem_clear(S["pick"])
                    step(v.tensor_copy(lists[:].unsqueeze(1), flat[:, ds(u, 1), :, :]))
                    step(*(v.max(top[:, q, best8], lists[:, q, :]) for q in range(2)))
                    step(*(v.max_index(picks[:, 2 + q, best8], top[:, q, best8], lists[:, q, :]) for q in range(2)),
                         *(v.match_replace(left[:, q, :], top[:, q, best8], lists[:, q, :], NEG) for q in range(2)))

                def second():
                    step(*(v.max(top[:, q, rest8], left[:, q, :]) for q in range(2)))
                    step(*(v.max_index(picks[:, 2 + q, rest8], top[:, q, rest8], left[:, q, :]) for q in range(2)),
                         v.tensor_tensor(cand[:], top[:, 0, :].unsqueeze(2).broadcast_to([P, TOPK, TOPK]),
                                         top[:, 1, :].unsqueeze(1).broadcast_to([P, TOPK, TOPK]), ALU.add))

                def third():
                    step(v.max(best[:, best8], flat_c))
                    step(v.max_index(pos[:, best8], best[:, best8], flat_c),
                         v.match_replace(flat_l, best[:, best8], flat_c, NEG))
                    step(v.max(best[:, rest8], flat_l))
                    step(v.max_index(pos[:, rest8], best[:, rest8], flat_l))
                    step(v.tensor_single_scalar(picks[:, 0, :], pos[:], 4, ALU.logical_shift_right),
                         v.tensor_single_scalar(picks[:, 1, :], pos[:], TOPK - 1, ALU.bitwise_and))
                    step(v.tensor_copy(picks_all[:, ds(u, 1), :, :], picks[:].unsqueeze(1)))
                    v.tensor_copy(best_all[:, ds(u, 1), :], best[:].unsqueeze(1)).then_inc(S["picked"], 1)

                return first, second, third

            low(0, 0)
            with dve.Fori(0, N1 // 3) as g:
                parts = [part for i in range(4) for part in pick(g * 4 + i)]
                for j in range(6):
                    low(1 - j % 2, g * 3 + (j // 2 + j % 2))
                    parts[2 * j]()
                    parts[2 * j + 1]()
            dve.wait_ge(S["picked"], NB * HEADS)
            with dve.Fori(0, N2) as b:
                n = [0]

                def step(ins):
                    n[0] += 1
                    ins.then_inc(S["l2_chain"], 1)
                    dve.wait_ge(S["l2_chain"], b * 3 + n[0])

                scores = best_all[:, ds(b * HEADS, HEADS), :]
                gates = sel[:, 2, :].rearrange("p (h k) -> p h k", h=HEADS)
                dve.wait_ge(S["selT_full"], b + PRIMED)
                nc.vector.tensor_tensor(gates, scores, best_all[:, ds(b * HEADS, HEADS), 0:1].broadcast_to([P, HEADS, TOPK]),
                                        ALU.subtract).then_inc(S["exp_in"], 1)
                low(1, b + N1)
                for q in range(2):
                    place = picks_all[:, ds(b * HEADS, HEADS), q, :].unsqueeze(3)
                    nc.vector.tensor_tensor(
                        eq[q][:].rearrange("p (h k) x -> p h k x", h=HEADS),
                        place.broadcast_to([P, HEADS, TOPK, TOPK]),
                        iota[:, 0:TOPK].unsqueeze(1).unsqueeze(1).broadcast_to([P, HEADS, TOPK, TOPK]),
                        ALU.is_equal).then_inc(eq_hot[q], 1)
                dve.wait_ge(S["exp_out"], b + 1)
                step(nc.vector.tensor_reduce(peak[:, 0, :], gates, X, ALU.add))
                step(nc.vector.reciprocal(peak[:, 1, :], peak[:, 0, :]))
                step(nc.vector.tensor_tensor(gates, gates, peak[:, 1, :].unsqueeze(2).broadcast_to([P, HEADS, TOPK]), ALU.mult))
                for q in range(2):
                    dve.wait_ge(eq_key[q], b + 1)
                    nc.vector.tensor_reduce(sel[:, q, :], eq[q][:], X, ALU.add).then_inc(S["sel_ready"], 1)
                low(0, b + (N1 + 1))
                dve.wait_ge(S["selT_full"], b + 1 + PRIMED)
                nc.vector.tensor_copy(selT[:, :, ds(b * P, P)],
                                      gp[0][:, 0:3 * P].rearrange("p (n t) -> p n t", n=3)).then_inc(S["selT_in"], 1)
            dve.wait_ge(S["selT_in"], NB + PRIMED)
            nc.vector.tensor_copy(gate_hi[:], selT[:, 2, :]).then_inc(S["gate_split"], 1)
            dve.wait_ge(S["gate_split"], 1)
            nc.vector.tensor_tensor(gate_lo[:], selT[:, 2, :], gate_hi[:].bitcast(F), ALU.subtract).then_inc(S["gate_split"], 1)
            dve.wait_ge(S["gate_split"], 2)
            with dve.Fori(0, N3 // 4) as q:
                for j in range(8):
                    s = j % 2
                    low(1 - s, q * 4 + (N1 + N2 + j // 2 + s))
                    dve.wait_ge(g_full[s], q * 4 + j // 2 + PRIMED)
                    nc.vector.tensor_tensor(hot[s][:, :, 0, :], selT[:, 0, ds(q * 64 + 8 * j, 8)].unsqueeze(2).broadcast_to([P, 8, KEYS]),
                                            iota[:].unsqueeze(1).broadcast_to([P, 8, KEYS]), ALU.is_equal)
                    for n in range(8):
                        t = q * 64 + (8 * j + n)
                        for part, gate in ((1, gate_hi[:].bitcast(F)), (2, gate_lo[:])):
                            last = nc.vector.tensor_scalar(hot[s][:, n, part, :], iota[:], selT[:, 1, ds(t, 1)],
                                                           gate[:, ds(t, 1)], ALU.is_equal, ALU.mult)
                    last.then_inc(hot_ready[s], 1)
            with dve.Fori(N1 + N2 + N3, KEYS // 2 - 1) as r:
                for s in range(2):
                    low(1 - s, r + s)
            low(1, KEYS // 2 - 1)


G4 = 4


def down_loads(sem, m, a, hd, gd):
    raw = [m.put(f"v_raw{i}", 52 + 16 * i, [P, G4, D]) for i in range(2)]
    hb = [m.put(f"dh{i}", 148 + 8 * i, [P, G4, T]) for i in range(2)]
    gb = [m.put(f"dg{i}", 164 + 8 * i, [P, T // 32, G4, 32]) for i in range(2)]
    v_in, g_in, h_in = ([sem(f"d_{n}{i}") for i in range(2)] for n in ("v_in", "g_in", "h_in"))
    vv = a["expert_v"][0].rearrange("(i r j) d -> i r (j d)", r=KEYS // G4, j=G4)
    hv = hd.rearrange("i (r j) t -> i r (j t)", j=G4)
    gv = gd.rearrange("b i (r x) -> i b r x", x=G4 * 32)

    def rows(eng, s, at):
        eng.dma_start(raw[s][:].rearrange("p j d -> p (j d)").unsqueeze(1), vv[:, at, :]).then_inc(v_in[s], 16)

    def weights(eng, s, at):
        eng.dma_start(hb[s][:].rearrange("p j t -> p (j t)").unsqueeze(1), hv[:, at, :]).then_inc(h_in[s], 16)
        eng.dma_start(gb[s][:].rearrange("p b j n -> p b (j n)"),
                      gv[:, :, at, :].rearrange("p b o x -> p b (o x)")).then_inc(g_in[s], 16)

    def first(eng, s, what):
        (rows, weights)[what](eng, s, slice(s, s + 1))

    return raw, hb, gb, v_in, g_in, h_in, rows, weights, first


def down_program(nc, sem, psum, m, a, acc, loads, out):
    raw, hb, gb, v_in, g_in, h_in, load_rows, load_weights, _ = loads
    ROUNDS = KEYS // G4 // 2
    wh = [m.put(f"dwh{i}", 16 + 8 * i, [P, G4, T], R) for i in range(2)]
    wl = [m.put(f"dwl{i}", 32 + 8 * i, [P, G4, T], R) for i in range(2)]
    vh = [m.put(f"vh{i}", 84 + 16 * i, [P, G4, D], R) for i in range(2)]
    vl = [m.put(f"vl{i}", 116 + 16 * i, [P, G4, D], R) for i in range(2)]
    fnorm = m.put("fnorm", 180, [P, D])
    fst = m.put("fst", 184, [P, 4, NB])
    ss, var, rs, tmp = (fst[:, i, :] for i in range(4))
    junk = m.put("junk", 148, [P, NB, D])

    v_hi, v_lo, w_f, w_hi, w_lo, o_full = (
        [sem(f"d_{n}{i}") for i in range(2)] for n in (
            "v_hi", "v_lo", "w_f", "w_hi", "w_lo", "o_full"))
    added = [sem(f"added{k}") for k in range(8)]
    S = {n: sem("d_" + n) for n in "fn_in sq root vchain normed out var".split()}

    with nc.Block() as block:
        @block.sync
        def _(sp_):
            for free in (*w_lo, *v_lo, *o_full, *added):
                sp_.sem_inc(free, PRIMED)
            sp_.dma_start(fnorm[:], a["final_norm"].unsqueeze(0).broadcast_to([P, D])).then_inc(S["fn_in"], 16)
            with sp_.Fori(1, ROUNDS) as r:
                for s in range(2):
                    sp_.wait_ge(w_lo[s], r + PRIMED)
                    load_weights(sp_, s, ds(r * 2 + s, 1))
                    sp_.wait_ge(v_lo[s], r + PRIMED)
                    load_rows(sp_, s, ds(r * 2 + s, 1))
            for b in range(NB):
                sp_.wait_ge(S["normed"], b + 1)
                sp_.dma_start(out[0, b * P:(b + 1) * P, :], acc[:, b, :]).then_inc(S["out"], 16)
            sp_.wait_ge(S["out"], NB * 16)

        @block.scalar
        def _(act):
            with act.Fori(0, ROUNDS) as r:
                for s in range(2):
                    act.wait_ge(v_in[s], r * 16 + 16)
                    act.wait_ge(o_full[s], r * 8 + PRIMED)
                    nc.scalar.activation(vh[s][:], raw[s][:], ACT.Copy).then_inc(v_hi[s], 1)
                    act.wait_ge(w_f[s], r + 1)
                    nc.scalar.activation(wh[s][:], hb[s][:], ACT.Copy).then_inc(w_hi[s], 1)
            for b in range(NB):
                act.wait_ge(added[2 * b + 1], ROUNDS * 2 + PRIMED)
                nc.scalar.activation(junk[:, b, :], acc[:, b, :], ACT.Square, accum_out=ss[:, b:b + 1]).then_inc(S["sq"], 1)
                act.wait_ge(S["var"], b + 1)
                nc.scalar.activation(rs[:, b:b + 1], var[:, b:b + 1], ACT.Sqrt).then_inc(S["root"], 1)

        @block.gpsimd
        def _(pool):
            with pool.Fori(0, ROUNDS) as r:
                for s in range(2):
                    pool.wait_ge(w_hi[s], r + 1)
                    nc.gpsimd.tensor_tensor(wl[s][:], hb[s][:], wh[s][:].bitcast(F), ALU.subtract).then_inc(w_lo[s], 1)

        @block.tensor
        def _(pe):
            with pe.Fori(0, ROUNDS) as r:
                for s in range(2):
                    pe.wait_ge(v_lo[s], r + 1 + PRIMED)
                    pe.wait_ge(w_lo[s], r + 1 + PRIMED)
                    for k in range(8):
                        b, half = k // 2, k % 2
                        pe.wait_ge(added[k], r * 2 + s + PRIMED)
                        for j in range(G4):
                            for n, (w, v) in enumerate(((wh, vh), (wh, vl), (wl, vh))):
                                last = nc.tensor.matmul(psum[k][:], w[s][:, j, b * P:(b + 1) * P],
                                                        v[s][:, j, half * T:(half + 1) * T],
                                                        start=(j == 0 and n == 0), stop=(j == G4 - 1 and n == 2))
                        last.then_inc(o_full[s], 1)

        @block.vector
        def _(dve):
            def prepare(s, r):
                dve.wait_ge(h_in[s], r * 16 + 16)
                dve.wait_ge(g_in[s], r * 16 + 16)
                w = hb[s][:].rearrange("p j (b n) -> p j b n", n=32)
                nc.vector.tensor_tensor(w, w, gb[s][:].rearrange("p b j n -> p j b n"), ALU.mult).then_inc(w_f[s], 1)
                dve.wait_ge(v_hi[s], r + 1)
                nc.vector.tensor_tensor(vl[s][:], raw[s][:], vh[s][:].bitcast(F), ALU.subtract).then_inc(v_lo[s], 1)

            def add(s, r, after=None):
                for k in range(8):
                    if after is not None and k % 2 == 0 and k:
                        after(k // 2 - 1)
                    b, half = k // 2, k % 2
                    dve.wait_ge(o_full[s], r * 8 + (k + 1) + PRIMED)
                    part = acc[:, b, half * T:(half + 1) * T]
                    nc.vector.tensor_tensor(part, part, psum[k][:], ALU.add).then_inc(added[k], 1)

            prepare(0, 0)
            with dve.Fori(0, ROUNDS - 1) as r:
                prepare(1, r)
                add(0, r)
                prepare(0, r + 1)
                add(1, r)
            prepare(1, ROUNDS - 1)
            add(0, ROUNDS - 1)
            done = [0]

            def chain(ins):
                done[0] += 1
                ins.then_inc(S["vchain"], 1)
                dve.wait_ge(S["vchain"], done[0])

            def norm_out(b):
                va, r, t = (x[:, b:b + 1] for x in (var, rs, tmp))
                dve.wait_ge(S["sq"], b + 1)
                nc.vector.tensor_scalar(va, ss[:, b:b + 1], 1.0 / D, EPS, ALU.mult, ALU.add).then_inc(S["var"], 1)
                dve.wait_ge(S["root"], b + 1)
                chain(nc.vector.reciprocal(r, r))
                chain(nc.vector.tensor_tensor(t, r, r, ALU.mult))
                chain(nc.vector.tensor_tensor(t, t, va, ALU.mult))
                chain(nc.vector.tensor_scalar(t, t, -0.5, 1.5, ALU.mult, ALU.add))
                chain(nc.vector.tensor_tensor(r, r, t, ALU.mult))
                nc.vector.scalar_tensor_tensor(acc[:, b, :], acc[:, b, :], r, fnorm[:], ALU.mult,
                                               ALU.mult).then_inc(S["normed"], 1)

            dve.wait_ge(S["fn_in"], 16)
            add(1, ROUNDS - 1, after=norm_out)
            norm_out(NB - 1)


def layer(nc, a, out):
    ctx = ExitStack()
    with ctx:
        def sem(name):
            return ctx.enter_context(nc.semaphore(name))

        psum = [ctx.enter_context(nc.psum_tensor(f"bank{i}", [P, T], F)) for i in range(8)]
        m = Map(nc, (nc.sbuf_base + 63) // 64 * 64)
        acc = m.put("acc", 0, [P, NB, D])
        sT = m.put("xTh", 16, [P, C, T], R), m.put("xTl", 32, [P, C, T], R)
        const = {n: m.put(n, 48 + i / 2, [P, P])
                 for i, n in enumerate(("ident", "iota", "tri", "ones", "causal", "gap"))}
        const["vecs"] = m.put("vecs", 51, [P, 32])
        hd = nc.dram_tensor("expert_act", (P, KEYS, T), F).ap()
        gd = nc.dram_tensor("expert_gate", (T // 32, P, KEYS * 32), F).ap()
        u_raw = [m.put(f"u_raw{i}", 100 + 4 * i, [P, D]) for i in range(2)]
        u_in = [sem(f"u_in{i}") for i in range(2)]
        u_view = a["expert_u"][0].rearrange("(i j) d -> i j d", j=KEYS)
        score = mix_program(nc, sem, psum, m, a, acc, sT, const, u_raw, u_in, u_view)
        loads = down_loads(sem, m, a, hd, gd)
        up_program(nc, sem, psum, m, a, sT, const, score, hd, gd, u_raw, u_in, u_view, loads[-1])
        down_program(nc, sem, psum, m, a, acc, loads, out)


_INS = ["x", "norm_mix", "w_in", "conv_w", "conv_b", "w_branch_a", "w_branch_b", "w_out", "norm_ffn", "w_q",
        "sub_keys", "expert_u", "expert_v", "final_norm"]


def kernel(**inputs):
    import concourse.bacc as _bacc
    from concourse.bass_utils import run_bass_kernel_spmd as _run

    nc = _bacc.Bacc("TRN2", target_bir_lowering=False, num_devices=1)
    arrays, a = {}, {}
    for name in _INS:
        x = np.ascontiguousarray(inputs[name])
        arrays[f"in_{name}"] = x
        a[name] = nc.dram_tensor(f"in_{name}", x.shape, mybir.dt.from_np(x.dtype), kind="ExternalInput").ap()
    out = nc.dram_tensor("out_0", (1, T, D), F, kind="ExternalOutput").ap()
    layer(nc, a, out)
    r = _run(nc, [arrays], core_ids=[0])
    return r.results[0]["out_0"]
```

```python
from contextlib import ExitStack

import numpy as np
import concourse.bass as bass
from concourse import mybir

F = mybir.dt.float32
R = mybir.dt.float32r
U32 = mybir.dt.uint32
ALU = mybir.AluOpType
ACT = mybir.ActivationFunctionType
X = mybir.AxisListType.X
ds = bass.ds

P = 128
T = 512
D = 1024
NB = T // P
C = D // P
SBW = 512
CW = 512
HEADS = 8
PAIRS = HEADS // 2
HD = 64
CT = CW // P
KEYS = 128
LISTS = 16
TOPK = 16
EPS = 1e-6
NEG = -3.0e38
FAR = -1.0e30
KB = 1024
PRIMED = 1

Q0, K0, V0 = 0, SBW, 2 * SBW
CB0, CC0, CU0 = 3 * SBW, 3 * SBW + CW, 3 * SBW + 2 * CW
GA0 = 3 * SBW + 3 * CW
GB0 = GA0 + D

ROW = {0: 0, 1: 512, 3: 896, 2: 1024}
ZW = 1280


class Map:

    def __init__(self, nc, base):
        self.nc, self.base = nc, base

    def put(self, name, kb, shape, dt=F):
        return self.nc.alloc_sbuf_tensor_at(name, shape, dt, offset=self.base + int(kb * KB))


def mix_program(nc, sem, psum, m, a, acc, sT, const, u_raw, u_in, u_view):
    ident, iota, tri, ones, causal, gap, vecs = (const[k] for k in (
        "ident", "iota", "tri", "ones", "causal", "gap", "vecs"))
    xh, xl = sT
    score = m.put("score", 52, [P, NB, LISTS, KEYS])
    ath = m.put("ath", 52, [P, PAIRS, T], R)
    atl = m.put("atl", 60, [P, PAIRS, T], R)
    cvh = m.put("cvh", 68, [P, CT, T], R)
    cvl = m.put("cvl", 76, [P, CT, T], R)
    mgh = m.put("mgh", 84, [P, C, T], R)
    mgl = m.put("mgl", 100, [P, C, T], R)
    xn = m.put("xn", 84, [P, NB, D])
    raw = [m.put(f"raw{i}", 116 + 4 * i, [P, C, P]) for i in range(3)]
    wh = [m.put(f"wh{i}", 128 + 4 * i, [P, C, P], R) for i in range(3)]
    wl = [m.put(f"wl{i}", 140 + 4 * i, [P, C, P], R) for i in range(3)]
    z = m.put("z", 152, [P, 2, ZW])
    sp = m.put("sp", 162, [P, 2, ZW])
    sph = m.put("sph", 94, [P, 2, ZW], R)
    spl = m.put("spl", 104, [P, 2, ZW], R)
    qT = m.put("qT", 172, [P, T])
    kT = m.put("kT", 174, [P, T])
    vT = m.put("vT", 176, [P, T])
    v = m.put("v", 178, [P, NB, P])
    cb = m.put("cb", 180, [P, T])
    cc = m.put("cc", 182, [P, T])
    cz = m.put("cz", 184, [P, 2 + T])
    cy = m.put("cy", 187, [P, T])
    ga = m.put("ga", 189, [P, T])
    gb = m.put("gb", 191, [P, T])
    ot = [m.put(f"ot{i}", 193 + 2 * i, [P, T]) for i in range(2)]
    keyT = m.put("keyT", 152, [P, LISTS, KEYS])
    key = m.put("key", 160, [P, LISTS, P])
    rows = m.put("rows", 197, [32, P])
    zeros = m.put("zeros", 199, [P, P])
    count = m.put("count", 199.5, [P, P], U32)
    squared = m.put("squared", 162, [P, NB, D])
    tri_r = m.put("tri_r", 200, [P, P], R)
    ones_r = m.put("ones_r", 200.5, [P, P], R)
    st = m.put("st", 198, [P, 5, NB])
    ss = st[:, 0:2, :]
    var, rs, tmp = (st[:, i, :] for i in range(2, 5))

    pj = psum[0:3]
    zt = psum[3:6]
    av = psum[6]
    tp = psum[7]

    S = {n: sem(n) for n in (
        "rows_in key_in sq_done var_ready root_ready xn_ready vec_T vec_in xT_full xT_hi xT_lo "
        "vT_full v_ready z_full z_copied abs_done soft_done sp_ready sp_hi sp_lo t_full "
        "t_used arg_ready att_ready av_full av_hi av_lo cv_y cv_hi cv_lo "
        "mg_sum mg_hi mg_lo oT_full x_added sum_consts xn_more scales "
        "key_T key_ready s_full s_out consts vchain vmax conv wcol made raw_b").split()}
    raw_in = [sem(f"raw_in{i}") for i in range(3)]
    w_hi = [sem(f"w_hi{i}") for i in range(3)]
    w_lo = [sem(f"w_lo{i}") for i in range(3)]
    tile_done = [sem(f"tile_done{i}") for i in range(3)]
    taken = [sem(f"taken{i}") for i in range(3)]

    x_in = [sem(f"x_in{b}") for b in range(NB)]
    nb_ring = [psum[3], psum[5], psum[6], psum[7]]
    w_in = a["w_in"][0].rearrange("(c p) f -> p c f", p=P)
    w_q = a["w_q"][0].rearrange("(c p) f -> p c f", p=P)
    w_o = a["w_out"][0].rearrange("(c p) f -> p c f", p=P)
    w_a = a["w_branch_a"][0].rearrange("(c p) f -> p c f", p=P)
    w_b = a["w_branch_b"][0].rearrange("(c p) f -> p c f", p=P)
    L4 = 16

    with nc.Block() as block:
        @block.sync
        def _(sp_):
            for free in (*w_lo, *(S[n] for n in ("t_used", "av_lo", "x_added", "s_out", "oT_full", "s_full"))):
                sp_.sem_inc(free, PRIMED)
            for b in range(NB):
                sp_.dma_start(acc[:, b, :], a["x"][0, b * P:(b + 1) * P, :]).then_inc(x_in[b], 16)
            for r0, n, src in ((0, C, a["norm_mix"][0].rearrange("(c p) -> c p", p=P)),
                               (8, C, a["norm_ffn"][0].rearrange("(c p) -> c p", p=P)),
                               (16, 12, a["conv_w"][0].rearrange("k o (t p) -> (k o t) p", p=P)),
                               (28, CT, a["conv_b"][0].rearrange("(t p) -> t p", p=P))):
                sp_.dma_start(rows[r0:r0 + n, :], src).then_inc(S["rows_in"], 16)

            def load(slot, r, src):
                sp_.wait_ge(S["rows_in"], 64)
                sp_.wait_ge(w_lo[slot], r + PRIMED)
                n = src.shape[1]
                sp_.dma_start(raw[slot][:, 0:n, :], src).then_inc(raw_in[slot], 16)

            with sp_.Fori(0, PAIRS) as p:
                for slot, f0 in enumerate((Q0, K0, V0)):
                    load(slot, p * 2, w_in[:, :, ds(p * P + f0, P)])
                for slot, f0 in enumerate((CB0, CC0, CU0)):
                    load(slot, p * 2 + 1, w_in[:, :, ds(p * P + f0, P)])
            with sp_.Fori(0, C) as c:
                load(0, c + 8, w_in[:, :, ds(c * P + GA0, P)])
                load(1, c + 8, w_in[:, :, ds(c * P + GB0, P)])
                load(2, c + 8, w_a[:, :, ds(c * P, P)])
                sp_.dma_start(raw[2][:, 4:8, :], w_b[:, :, ds(c * P, P)]).then_inc(S["raw_b"], 16)
            sp_.wait_ge(S["av_hi"], PAIRS)
            sp_.dma_start(key[:], a["sub_keys"][0].rearrange("h q k c -> k (h q) c")).then_inc(S["key_in"], 16)
            with sp_.Fori(0, C // 2) as i:
                for slot in range(2):
                    load(slot, i + L4, w_o[:, :, ds(i * 2 * P + slot * P, P)])
            with sp_.Fori(0, LISTS // 2) as i:
                for slot in range(2):
                    load(slot, i + (L4 + C // 2), w_q[:, :, ds(i * 2 * P + slot * P, P)])
            sp_.wait_ge(S["x_added"], C + PRIMED)
            for i in range(2):
                sp_.dma_start(u_raw[i][:].unsqueeze(1), u_view[:, i:i + 1, :]).then_inc(u_in[i], 16)

        @block.gpsimd
        def _(pool):
            nc.gpsimd.memset(ones[:], 1.0)
            nc.gpsimd.memset(zeros[:], 0.0)
            nc.gpsimd.iota(count[:], pattern=[[1, P]], base=0, channel_multiplier=0).then_inc(S["made"], 1)
            pool.wait_ge(S["made"], 1)
            nc.gpsimd.tensor_copy(iota[:], count[:])
            for out_, in_, op, fill, step, per in (
                    (ident, zeros, ALU.not_equal, 1.0, -1, 1),
                    (tri, ones, ALU.is_ge, 0.0, -1, 1),
                    (causal, ones, ALU.is_gt, 0.0, 1, -1),
                    (gap, zeros, ALU.is_gt, FAR, 1, -1)):
                last = nc.gpsimd.affine_select(out=out_[:], in_=in_[:], compare_op=op, fill=fill, base=0,
                                               pattern=[[step, P]], channel_multiplier=per)
            last.then_inc(S["consts"], 1)
            pool.wait_ge(S["consts"], 1)
            nc.gpsimd.tensor_copy(tri_r[:], tri[:])
            nc.gpsimd.tensor_copy(ones_r[:], ones[:]).then_inc(S["sum_consts"], 1)

            def split(slot, r):
                pool.wait_ge(w_hi[slot], r + 1)
                nc.gpsimd.tensor_tensor(wl[slot][:], raw[slot][:], wh[slot][:].bitcast(F),
                                        ALU.subtract).then_inc(w_lo[slot], 1)

            with pool.Fori(0, PAIRS + CT) as r:
                for slot in range(3):
                    split(slot, r)
            with pool.Fori(0, C) as c:
                for slot in range(3):
                    split(slot, c + (PAIRS + CT))
            with pool.Fori(L4, L4 + 12) as r:
                for slot in range(2):
                    split(slot, r)

        @block.tensor
        def _(pe):
            def chunk(out, slot, hi, lo, i, at, first, last):
                for n, (w, x) in enumerate(((wh, hi), (wh, lo), (wl, hi))):
                    done = nc.tensor.matmul(out, w[slot][:, at, :], x[:, i, :],
                                            start=(first and n == 0), stop=(last and n == 2))
                return done

            def three_pass(out, slot, hi, lo, chunks, w0=0):
                for i in range(chunks):
                    last = chunk(out, slot, hi, lo, i, w0 + i, i == 0, i == chunks - 1)
                return last

            def project(slot, r, hi, lo):
                pe.wait_ge(w_lo[slot], r + 1 + PRIMED)
                pe.wait_ge(taken[slot], r)
                three_pass(pj[slot][:], slot, hi, lo, C).then_inc(tile_done[slot], 1)

            def norm_project(first, n0, r):
                ring = len(nb_ring)
                pe.wait_ge(S["xn_ready"], n0 // 2)
                pe.wait_ge(S["xn_more"], n0 // 2)
                for c in range(C + ring - 1):
                    done = c - (ring - 1)
                    if done >= 0:
                        pe.wait_ge(S["xT_lo"], first + done + 1)
                    if c < C:
                        for b in range(NB):
                            last = nc.tensor.transpose(nb_ring[c % ring][:, b * P:(b + 1) * P],
                                                       xn[:, b, c * P:(c + 1) * P], ident[:])
                        last.then_inc(S["xT_full"], 1)
                    if done == 0:
                        pe.wait_ge(w_lo[0], r + 1 + PRIMED)
                        pe.wait_ge(taken[0], r)
                    if done >= 0:
                        last = chunk(pj[0][:], 0, xh, xl, done, done, done == 0, done == C - 1)
                last.then_inc(tile_done[0], 1)

            def scores(p, e):
                pe.wait_ge(taken[1], p * 2 + 1)
                if e == 0:
                    pe.wait_ge(S["t_used"], p * 2 + PRIMED)
                else:
                    pe.wait_ge(S["z_copied"], p * 2 + 1)
                h = slice(e * HD, (e + 1) * HD)
                for kb, o in ROW.items():
                    last = nc.tensor.matmul(zt[o // T][:, o % T:o % T + T - kb * P], kT[h, kb * P:(kb + 1) * P],
                                            qT[h, kb * P:], start=True, stop=True)
                last.then_inc(S["z_full"], 1)

            def sums(p, e):
                pe.wait_ge(S["sp_lo"], p * 2 + e + 1)
                pe.wait_ge(S["z_copied"], p * 2 + 2)
                pe.wait_ge(S["t_used"], p * 2 + e + PRIMED)
                for kb, o in ROW.items():
                    for jb in range(kb, NB):
                        for half in (sph, spl):
                            last = nc.tensor.matmul(
                                zt[o // T][:, o % T + (jb - kb) * P:o % T + T - kb * P], (tri_r if jb == kb else ones_r)[:],
                                half[:, e, ROW[jb]:ROW[jb] + T - jb * P], start=(jb == kb and half is sph),
                                stop=(jb == NB - 1 and half is spl))
                last.then_inc(S["t_full"], 1)

            def outputs(p):
                pe.wait_ge(S["av_lo"], p + PRIMED)
                pe.wait_ge(S["v_ready"], p + 1)
                for e in range(2):
                    h = slice(e * HD, (e + 1) * HD)
                    pe.wait_ge(S["att_ready"], p * 2 + e + 1)
                    for kb in range(NB):
                        last = nc.tensor.matmul(av[h, kb * P:], v[:, kb, h], z[:, e, ROW[kb]:ROW[kb] + T - kb * P],
                                                start=(kb == 0), stop=(kb == NB - 1))
                last.then_inc(S["av_full"], 1)

            def transpose_v(p):
                pe.wait_ge(taken[2], p * 2 + 1)
                for b in range(NB):
                    last = nc.tensor.transpose(tp[:, b * P:(b + 1) * P], vT[:, b * P:(b + 1) * P], ident[:])
                last.then_inc(S["vT_full"], 1)

            pe.wait_ge(S["consts"], 1)
            pe.wait_ge(S["rows_in"], 64)
            nc.tensor.transpose(pj[0][:, 0:32], rows[:, :], ident[0:32, 0:32]).then_inc(S["vec_T"], 1)
            pe.wait_ge(S["vec_in"], 1)
            norm_project(0, NB, 0)

            def pair(p, r, before=None):
                if before is not None:
                    project(0, r, xh, xl)
                    sums(before, 0)
                project(1, r, xh, xl)
                if before is not None:
                    sums(before, 1)
                project(2, r, xh, xl)
                if before is not None:
                    outputs(before)
                scores(p, 0)
                project(0, r + 1, xh, xl)
                transpose_v(p)
                scores(p, 1)
                project(1, r + 1, xh, xl)
                project(2, r + 1, xh, xl)

            pair(0, 0)
            pe.wait_ge(S["sum_consts"], 1)
            with pe.Fori(1, PAIRS) as p:
                pair(p, p * 2, before=p - 1)

            def gated(r, before=None):
                project(0, r, xh, xl)
                if before is not None:
                    sums(before, 0)
                project(1, r, xh, xl)
                if before is not None:
                    sums(before, 1)
                    outputs(before)
                pe.wait_ge(S["av_lo"], PAIRS + PRIMED)
                pe.wait_ge(S["cv_lo"], CT)
                pe.wait_ge(w_lo[2], r + 1 + PRIMED)
                pe.wait_ge(taken[2], r)
                three_pass(pj[2][:], 2, ath, atl, 4)
                three_pass(zt[0][:], 2, cvh, cvl, 4, w0=4).then_inc(tile_done[2], 1)

            gated(PAIRS * 2, before=PAIRS - 1)
            with pe.Fori(PAIRS * 2 + 1, L4) as r:
                gated(r)
            def transpose_keys(g):
                for q in range(4):
                    last = nc.tensor.transpose(zt[1 + g % 2][:, q * P:(q + 1) * P], key[:, 4 * g + q, :], ident[:])
                last.then_inc(S["key_T"], 1)

            def transpose_out(slot, i):
                pe.wait_ge(taken[slot], i + (L4 + 1))
                pe.wait_ge(S["x_added"], i * 2 + slot + PRIMED)
                for b in range(NB):
                    last = nc.tensor.transpose(tp[:, b * P:(b + 1) * P], ot[slot][:, b * P:(b + 1) * P], ident[:])
                last.then_inc(S["oT_full"], 1)

            pe.wait_ge(w_lo[0], L4 + 1 + PRIMED)
            pe.wait_ge(taken[0], L4)
            pe.wait_ge(S["mg_lo"], C - 1)
            for c in range(C):
                if c == C - 1:
                    pe.wait_ge(S["key_in"], 16)
                    transpose_keys(0)
                    transpose_keys(1)
                    pe.wait_ge(S["mg_lo"], C)
                last = chunk(pj[0][:], 0, mgh, mgl, c, c, c == 0, c == C - 1)
            last.then_inc(tile_done[0], 1)
            with pe.Fori(0, C // 2 - 1) as i:
                project(1, i + L4, mgh, mgl)
                transpose_out(0, i)
                project(0, i + (L4 + 1), mgh, mgl)
                transpose_out(1, i)
            pe.wait_ge(S["key_ready"], 2)
            transpose_keys(2)
            transpose_keys(3)
            project(1, L4 + C // 2 - 1, mgh, mgl)
            transpose_out(0, C // 2 - 1)
            transpose_out(1, C // 2 - 1)
            pe.wait_ge(S["key_ready"], LISTS // 4)

            def score_list(slot, i):
                pe.wait_ge(taken[slot], i + (L4 + C // 2 + 1))
                pe.wait_ge(S["s_out"], i * 2 + PRIMED)
                at = slice(i * 2 + slot, i * 2 + slot + 1) if isinstance(i, int) else ds(i * 2 + slot, 1)
                for b in range(NB):
                    last = nc.tensor.matmul(zt[slot][:, b * P:(b + 1) * P], ot[slot][:, b * P:(b + 1) * P],
                                            keyT[:, at, :], start=True, stop=True)
                last.then_inc(S["s_full"], 1)

            L5 = L4 + C // 2
            norm_project(C, 2 * NB, L5)
            with pe.Fori(0, LISTS // 2 - 1) as i:
                project(1, i + L5, xh, xl)
                score_list(0, i)
                project(0, i + (L5 + 1), xh, xl)
                score_list(1, i)
            project(1, L5 + LISTS // 2 - 1, xh, xl)
            score_list(0, LISTS // 2 - 1)
            score_list(1, LISTS // 2 - 1)

        @block.scalar
        def _(act):
            def squares(half, columns):
                for b in range(NB):
                    nc.scalar.activation(squared[:, b, columns], acc[:, b, columns], ACT.Square,
                                         accum_out=ss[:, half, b:b + 1]).then_inc(S["sq_done"], 1)

            def normed(first):
                act.wait_ge(S["var_ready"], first + 1)
                nc.scalar.activation(rs, var, ACT.Sqrt).then_inc(S["root_ready"], 1)
                act.wait_ge(S["scales"], first + 1)
                for b in range(NB // 2, NB):
                    nc.scalar.activation(xn[:, b, :], acc[:, b, :], ACT.Copy, scale=rs[:, b:b + 1]).then_inc(S["xn_more"], 1)

            def norm_hi(first, gain):
                for c in range(C):
                    act.wait_ge(S["xT_full"], first + c + 1)
                    nc.scalar.activation(xh[:, c, :], nb_ring[c % 4][:], ACT.Copy,
                                         scale=vecs[:, gain + c:gain + c + 1]).then_inc(S["xT_hi"], 1)

            def copy_scores(p, e):
                act.wait_ge(S["z_full"], p * 2 + e + 1)
                for b, n in enumerate((T, T, ZW - 2 * T)):
                    last = nc.scalar.activation(z[:, e, b * T:b * T + n], zt[b][:, 0:n], ACT.Copy)
                last.then_inc(S["z_copied"], 1)

            def softplus(p, e):
                act.wait_ge(S["abs_done"], p * 2 + e + 1)
                nc.scalar.activation(sp[:, e, :], sp[:, e, :], ACT.Exp, scale=-1.0).then_inc(S["soft_done"], 1)
                act.wait_ge(S["soft_done"], p * 4 + 2 * e + 1)
                nc.scalar.activation(sp[:, e, :], sp[:, e, :], ACT.Ln, bias=1.0).then_inc(S["soft_done"], 1)

            def softplus_hi(p, e):
                act.wait_ge(S["sp_ready"], p * 2 + e + 1)
                nc.scalar.activation(sph[:, e, :], sp[:, e, :], ACT.Copy).then_inc(S["sp_hi"], 1)

            def exps(p, e):
                act.wait_ge(S["arg_ready"], p * 2 + e + 1)
                nc.scalar.activation(z[:, e, :], z[:, e, :], ACT.Exp).then_inc(S["att_ready"], 1)

            def attention_hi(p):
                act.wait_ge(S["av_full"], p + 1)
                nc.scalar.activation(ath[:, ds(p, 1), :] if not isinstance(p, int) else ath[:, p:p + 1, :],
                                     av[:], ACT.Copy).then_inc(S["av_hi"], 1)

            def take(slot, r, out, func=ACT.Copy, scale=1.0):
                act.wait_ge(tile_done[slot], r + 1)
                nc.scalar.activation(out, pj[slot][:], func, scale=scale).then_inc(taken[slot], 1)

            def high(slot, r):
                act.wait_ge(raw_in[slot], r * 16 + 16)
                act.wait_ge(tile_done[slot], r)
                nc.scalar.activation(wh[slot][:], raw[slot][:], ACT.Copy).then_inc(w_hi[slot], 1)

            def both_highs(c):
                act.wait_ge(S["raw_b"], c * 16 + 16)
                high(2, c + (PAIRS + CT))

            nc.scalar.preload_act_table_set("sqrt_and_others")
            for b in range(NB):
                act.wait_ge(x_in[b], 16)
                nc.scalar.activation(squared[:, b, :], acc[:, b, :], ACT.Square,
                                     accum_out=ss[:, 0, b:b + 1]).then_inc(S["sq_done"], 1)
            normed(0)
            high(0, 0)
            high(1, 0)
            nc.scalar.preload_act_table_set("natural_log_exp_and_others")
            norm_hi(0, 0)

            def conv_hi(t):
                at = slice(t, t + 1) if isinstance(t, int) else ds(t, 1)
                act.wait_ge(S["cv_y"], t + 1)
                nc.scalar.activation(cvh[:, at, :], cy[:].unsqueeze(1), ACT.Copy).then_inc(S["cv_hi"], 1)

            def pair(p, r, before=None):
                high(2, r)
                take(0, r, qT[:], scale=HD ** -0.5)
                high(0, r + 1)
                take(1, r, kT[:])
                high(1, r + 1)
                if before is not None:
                    exps(before, 0)
                    exps(before, 1)
                take(2, r, vT[:])
                high(2, r + 1)
                if before is not None:
                    attention_hi(before)
                copy_scores(p, 0)
                take(0, r + 1, cb[:])
                high(0, r + 2)
                softplus(p, 0)
                copy_scores(p, 1)
                softplus_hi(p, 0)
                softplus(p, 1)
                softplus_hi(p, 1)
                take(1, r + 1, cc[:])
                high(1, r + 2)
                conv_hi(p)

            pair(0, 0)
            with act.Fori(1, PAIRS) as p:
                pair(p, p * 2, before=p - 1)
            R0 = PAIRS * 2

            def gated(r, c, before=None):
                both_highs(c)
                if before is not None:
                    high(0, r + 1)
                    exps(before, 0)
                    high(1, r + 1)
                    exps(before, 1)
                    attention_hi(before)
                    nc.scalar.preload_act_table_set("sigmoid_and_others")
                    take(0, r, ga[:], ACT.Sigmoid)
                    take(1, r, gb[:], ACT.Sigmoid)
                else:
                    take(0, r, ga[:], ACT.Sigmoid)
                    high(0, r + 1)
                    take(1, r, gb[:], ACT.Sigmoid)
                    high(1, r + 1)
                at = slice(c, c + 1) if isinstance(c, int) else ds(c, 1)
                act.wait_ge(S["mg_sum"], c + 1)
                nc.scalar.activation(mgh[:, at, :], ga[:].unsqueeze(1), ACT.Copy).then_inc(S["mg_hi"], 1)
                act.wait_ge(S["mg_lo"], c + 1)

            gated(R0, 0, before=PAIRS - 1)
            with act.Fori(R0 + 1, L4) as r:
                gated(r, r - R0)

            def take_keys(g):
                act.wait_ge(S["key_T"], g + 1)
                nc.scalar.activation(keyT[:, 4 * g:4 * g + 4, :], zt[1 + g % 2][:], ACT.Copy).then_inc(S["key_ready"], 1)

            take_keys(0)
            take_keys(1)
            with act.Fori(0, C // 2 - 1) as i:
                for slot in range(2):
                    act.wait_ge(S["oT_full"], i * 2 + PRIMED)
                    take(slot, i + L4, ot[slot][:])
                    high(slot, i + (L4 + 1))
            take_keys(2)
            take_keys(3)
            nc.scalar.preload_act_table_set("sqrt_and_others")
            act.wait_ge(S["x_added"], C - 2 + PRIMED)
            squares(0, slice(0, D - 2 * P))
            act.wait_ge(S["oT_full"], C - 2 + PRIMED)
            take(0, L4 + C // 2 - 1, ot[0][:])
            high(0, L4 + C // 2)
            take(1, L4 + C // 2 - 1, ot[1][:])
            act.wait_ge(S["x_added"], C + PRIMED)
            squares(1, slice(D - 2 * P, D))
            normed(1)
            high(1, L4 + C // 2)
            norm_hi(C, C)

            def take_query(i, slot):
                act.wait_ge(S["s_full"], i * 2 + PRIMED)
                take(slot, i + (L4 + C // 2), ot[slot][:])

            with act.Fori(0, LISTS // 2 - 1) as i:
                for slot in range(2):
                    take_query(i, slot)
                    high(slot, i + (L4 + C // 2 + 1))
            for slot in range(2):
                take_query(LISTS // 2 - 1, slot)
            nc.scalar.preload_act_table_set("gelu_and_others")

        @block.vector
        def _(dve):
            done = [0]

            def chain(ins):
                done[0] += 1
                ins.then_inc(S["vchain"], 1)
                dve.wait_ge(S["vchain"], done[0])

            def normed(first):
                if first == 0:
                    dve.wait_ge(S["sq_done"], NB)
                else:
                    dve.wait_ge(S["sq_done"], 3 * NB)
                    chain(nc.vector.tensor_tensor(ss[:, 0, :], ss[:, 0, :], ss[:, 1, :], ALU.add))
                nc.vector.tensor_scalar(var, ss[:, 0, :], 1.0 / D, EPS, ALU.mult, ALU.add).then_inc(S["var_ready"], 1)
                dve.wait_ge(S["root_ready"], first + 1)
                chain(nc.vector.reciprocal(rs, rs))
                chain(nc.vector.tensor_tensor(tmp, rs, rs, ALU.mult))
                chain(nc.vector.tensor_tensor(tmp, tmp, var, ALU.mult))
                chain(nc.vector.tensor_scalar(tmp, tmp, -0.5, 1.5, ALU.mult, ALU.add))
                nc.vector.tensor_tensor(rs, rs, tmp, ALU.mult).then_inc(S["scales"], 1)
                dve.wait_ge(S["scales"], first + 1)
                for b in range(NB // 2):
                    nc.vector.tensor_scalar(xn[:, b, :], acc[:, b, :], rs[:, b:b + 1], None,
                                            ALU.mult).then_inc(S["xn_ready"], 1)

            def norm_lo(first, gain):
                for c in range(C):
                    dve.wait_ge(S["xT_hi"], first + c + 1)
                    nc.vector.scalar_tensor_tensor(xl[:, c, :], nb_ring[c % 4][:], vecs[:, gain + c:gain + c + 1],
                                                   xh[:, c, :].bitcast(F), ALU.mult,
                                                   ALU.subtract).then_inc(S["xT_lo"], 1)

            chain(nc.vector.memset(cz[:, 0:2], 0.0))
            dve.wait_ge(S["vec_T"], 1)
            nc.vector.tensor_copy(vecs[:], pj[0][:, 0:32]).then_inc(S["vec_in"], 1)
            dve.wait_ge(S["vec_in"], 1)
            normed(0)
            norm_lo(0, 0)

            def take_v(p):
                dve.wait_ge(S["vT_full"], p + 1)
                nc.vector.tensor_copy(v[:], tp[:].rearrange("p (b f) -> p b f", b=NB)).then_inc(S["v_ready"], 1)

            def diagonals(x, e):
                return (x[:, e, 0:2 * T].rearrange("p (b q) -> p b q", b=2)[:, :, 0:P],
                        x[:, e, ROW[3]:ROW[3] + 2 * P].rearrange("p (b q) -> p b q", b=2))

            def wide(mask):
                return mask[:].unsqueeze(1).broadcast_to([P, 2, P])

            def magnitudes(p, e):
                dve.wait_ge(S["z_copied"], p * 2 + e + 1)
                nc.vector.scalar_tensor_tensor(sp[:, e, :], z[:, e, :], -1.0, z[:, e, :], ALU.mult,
                                               ALU.max).then_inc(S["abs_done"], 1)

            def soft(p, e):
                dve.wait_ge(S["soft_done"], p * 4 + 2 * e + 2)
                nc.vector.scalar_tensor_tensor(sp[:, e, :], z[:, e, :], 0.0, sp[:, e, :], ALU.max,
                                               ALU.add).then_inc(S["vmax"], 1)
                dve.wait_ge(S["vmax"], p * 2 + e + 1)
                for part in diagonals(sp, e):
                    last = nc.vector.tensor_tensor(part, part, wide(causal), ALU.mult)
                last.then_inc(S["sp_ready"], 1)

            def soft_lo(p, e):
                dve.wait_ge(S["sp_hi"], p * 2 + e + 1)
                nc.vector.tensor_tensor(spl[:, e, :], sp[:, e, :], sph[:, e, :].bitcast(F), ALU.subtract).then_inc(S["sp_lo"], 1)

            def arguments(p):
                for e in range(2):
                    dve.wait_ge(S["t_full"], p * 2 + e + 1)
                    for b, n in enumerate((T, T, ZW - 2 * T)):
                        last = nc.vector.tensor_tensor(z[:, e, b * T:b * T + n], z[:, e, b * T:b * T + n],
                                                       zt[b][:, 0:n], ALU.subtract)
                    last.then_inc(S["t_used"], 1)
                    dve.wait_ge(S["t_used"], p * 2 + e + 1 + PRIMED)
                    for part in diagonals(z, e):
                        last = nc.vector.scalar_tensor_tensor(part, part, 0.0, wide(gap), ALU.min, ALU.add)
                    last.then_inc(S["arg_ready"], 1)

            def attention_lo(p):
                dve.wait_ge(S["av_hi"], p + 1)
                at = slice(p, p + 1) if isinstance(p, int) else ds(p, 1)
                nc.vector.tensor_tensor(atl[:, at, :], av[:].unsqueeze(1), ath[:, at, :].bitcast(F),
                                        ALU.subtract).then_inc(S["av_lo"], 1)

            wcol = m.put("wcol", 198.5, [P, 4])

            def convolve(t):
                def step(n, ins):
                    ins.then_inc(S["conv"], 1)
                    dve.wait_ge(S["conv"], t * 3 + n)
                cols = vecs[:, 16:32].rearrange("p (k t) -> p k t", k=4)
                at = slice(t, t + 1) if isinstance(t, int) else ds(t, 1)
                nc.vector.tensor_copy(wcol[:].unsqueeze(2), cols[:, :, at]).then_inc(S["wcol"], 1)
                dve.wait_ge(S["wcol"], t + 1)
                dve.wait_ge(taken[1], t * 2 + 2)
                dve.wait_ge(tile_done[2], t * 2 + 2)
                nc.vector.tensor_tensor(cz[:, 2:2 + T], pj[2][:], cc[:], ALU.mult).then_inc(taken[2], 1)
                dve.wait_ge(taken[2], t * 2 + 2)
                step(1, nc.vector.tensor_scalar(cy[:], cz[:, 2:2 + T], wcol[:, 2:3], wcol[:, 3:4], ALU.mult, ALU.add))
                step(2, nc.vector.scalar_tensor_tensor(cy[:], cz[:, 1:1 + T], wcol[:, 1:2], cy[:], ALU.mult, ALU.add))
                step(3, nc.vector.scalar_tensor_tensor(cy[:], cz[:, 0:T], wcol[:, 0:1], cy[:], ALU.mult, ALU.add))
                nc.vector.tensor_tensor(cy[:], cy[:], cb[:], ALU.mult).then_inc(S["cv_y"], 1)
                dve.wait_ge(S["cv_hi"], t + 1)
                nc.vector.tensor_tensor(cvl[:, at, :], cy[:].unsqueeze(1), cvh[:, at, :].bitcast(F),
                                        ALU.subtract).then_inc(S["cv_lo"], 1)

            def pair(p, before=None):
                if before is not None:
                    arguments(before)
                    attention_lo(before)
                magnitudes(p, 0)
                take_v(p)
                soft(p, 0)
                magnitudes(p, 1)
                soft_lo(p, 0)
                soft(p, 1)
                soft_lo(p, 1)
                convolve(p)

            pair(0)
            with dve.Fori(1, PAIRS) as p:
                pair(p, before=p - 1)
            arguments(PAIRS - 1)
            attention_lo(PAIRS - 1)

            with dve.Fori(0, C) as c:
                dve.wait_ge(taken[1], c + (PAIRS + CT + 1))
                dve.wait_ge(tile_done[2], c + (PAIRS + CT + 1))
                nc.vector.tensor_tensor(gb[:], gb[:], zt[0][:], ALU.mult)
                nc.vector.tensor_tensor(ga[:], ga[:], pj[2][:], ALU.mult).then_inc(taken[2], 1)
                dve.wait_ge(taken[2], c + (PAIRS + CT + 1))
                nc.vector.tensor_tensor(ga[:], ga[:], gb[:], ALU.add).then_inc(S["mg_sum"], 1)
                dve.wait_ge(S["mg_hi"], c + 1)
                nc.vector.tensor_tensor(mgl[:, ds(c, 1), :], ga[:].unsqueeze(1), mgh[:, ds(c, 1), :].bitcast(F),
                                        ALU.subtract).then_inc(S["mg_lo"], 1)

            with dve.Fori(0, C) as c:
                dve.wait_ge(S["oT_full"], c + 1 + PRIMED)
                part = acc[:, :, ds(c * P, P)]
                nc.vector.tensor_tensor(part, part, tp[:].rearrange("p (b f) -> p b f", b=NB),
                                        ALU.add).then_inc(S["x_added"], 1)
            normed(1)
            norm_lo(C, C)
            with dve.Fori(0, LISTS // 2) as i:
                for slot in range(2):
                    dve.wait_ge(S["s_full"], i * 2 + slot + 1 + PRIMED)
                    nc.vector.tensor_copy(score[:, :, ds(i * 2 + slot, 1), :],
                                          zt[slot][:].rearrange("p (b o k) -> p b o k", b=NB, o=1)).then_inc(S["s_out"], 1)
    return score


def up_program(nc, sem, psum, m, sT, const, score, hd, gd, raw, u_in, u_view, down):
    ident, iota = const["ident"], const["iota"]
    xh, xl = sT
    uh = [m.put(f"uh{i}", 84 + 4 * i, [P, C, P], R) for i in range(2)]
    ul = [m.put(f"ul{i}", 92 + 4 * i, [P, C, P], R) for i in range(2)]
    hb = [m.put(f"hb{i}", 108 + 2 * i, [P, T]) for i in range(2)]
    grid = [m.put(f"grid{i}", 112 + 16 * i, [P, KEYS, 32]) for i in range(2)]
    lists = m.put("lists", 112, [P, 2, 2, KEYS])
    left = m.put("left", 114, [P, 2, 2, KEYS])
    cand = m.put("cand", 116, [P, 2, TOPK, TOPK])
    cleft = m.put("cleft", 118, [P, 2, TOPK, TOPK])
    top = m.put("top", 120, [P, 2, 2, TOPK])
    best = m.put("best", 121, [P, 2, TOPK])
    pos = m.put("pos", 122, [P, 2, TOPK], U32)
    picks = m.put("picks", 123, [P, 2, 4, TOPK], U32)
    best_all = m.put("best_all", 150, [P, NB * HEADS, TOPK])
    picks_all = m.put("picks_all", 152, [P, NB * HEADS, 4, TOPK])
    sel = m.put("sel", 187, [P, NB, 3, HEADS * TOPK])
    total = m.put("total", 160, [P, 2, NB * HEADS])
    selT = m.put("selT", 163, [P, 2, T])
    eq = [m.put(f"eq{i}", 170 + 8 * i, [P, HEADS * TOPK, TOPK]) for i in range(2)]
    hot = [m.put(f"hot{i}", 170 + 12 * i, [P, 8, 3, KEYS], R) for i in range(2)]
    gate_hi = m.put("gate_hi", 194, [P, T], R)
    gate_lo = m.put("gate_lo", 196, [P, T])

    parts = [m.put(f"parts{i}", 144 + 8 * i, [P, 8, 2, KEYS]) for i in range(2)]

    utp = psum[0:2]
    zb = psum[4:6]
    gp = [psum[i] for i in (6, 7, 2, 3)]

    ut_full, ut_hi, ut_lo, u_mm, h_done, h_out, hot_ready, g_full, g_sum, g_out = (
        [sem(f"{n}{i}") for i in range(2)] for n in (
            "ut_full", "ut_hi", "ut_lo", "u_mm", "h_done", "h_out", "hot_ready", "g_full", "g_sum", "g_out"))
    S = {n: sem(n) for n in ("pick picked exp_in exp_out sel_ready selT_full selT_in "
                             "gate_norm g_evac gate_split").split()}
    eq_hot, eq_key = [sem(f"eq_hot{i}") for i in range(2)], [sem(f"eq_key{i}") for i in range(2)]
    hv = hd.rearrange("i (r s) t -> i r s t", s=2)
    uv = u_view.rearrange("i (r s) d -> i r s d", s=2)

    N1, N2, N3, N4 = 20, 6, 32, 6
    assert N1 + N2 + N3 + N4 == KEYS // 2

    with nc.Block() as block:
        @block.sync
        def _(sp_):
            for free in (*ut_full, *ut_lo, *h_done, *u_mm, *g_full, *g_sum, S["g_evac"], S["sel_ready"],
                         *down.v_lo, *down.w_lo):
                sp_.sem_inc(free, PRIMED)
            for free in (*h_out, *g_out):
                sp_.sem_inc(free, PRIMED * 16)

            def load(r):
                for s in range(2):
                    sp_.wait_ge(ut_full[s], r + PRIMED)
                    sp_.dma_start(raw[s][:].unsqueeze(1), uv[:, ds(r, 1), s, :]).then_inc(u_in[s], 16)

            with sp_.Fori(1, KEYS // 2 - N4) as r:
                load(r)
            sp_.wait_ge(S["picked"], NB * HEADS)
            for s in range(2):
                down.load_rows(sp_, s, slice(s, s + 1))
                sp_.wait_ge(h_out[s], (4 + PRIMED) * 16)
            down.load_acts(sp_, 0, slice(0, 1))
            with sp_.Fori(KEYS // 2 - N4, KEYS // 2) as r:
                load(r)
            for half in range(2):
                sp_.wait_ge(g_out[half], (N3 // 4 + PRIMED) * 16)
            down.load_gates(sp_, 0, slice(0, 1))
            down.load_acts(sp_, 1, slice(1, 2))
            down.load_gates(sp_, 1, slice(1, 2))

        @block.tensor
        def _(pe):
            def transposes(s, r):
                pe.wait_ge(u_in[s], r * 16 + 16)
                pe.wait_ge(ut_lo[1 - s], r + (s + PRIMED))
                for c in range(C):
                    last = nc.tensor.transpose(utp[c // 4][:, c % 4 * P:(c % 4 + 1) * P],
                                               raw[s][:, c * P:(c + 1) * P], ident[:])
                last.then_inc(ut_full[s], 1)

            def products(s, r):
                pe.wait_ge(ut_lo[s], r + 1 + PRIMED)
                pe.wait_ge(h_done[s], r + PRIMED)
                for c in range(C):
                    for n, (w, x) in enumerate(((uh, xh), (uh, xl), (ul, xh))):
                        last = nc.tensor.matmul(zb[s][:], w[s][:, c, :], x[:, c, :],
                                                start=(c == 0 and n == 0), stop=(c == C - 1 and n == 2))
                last.then_inc(u_mm[s], 1)

            def step(s, r, ahead=True):
                if ahead:
                    transposes(1 - s, r + s)
                products(s, r)

            def spread(s, r, k):
                pe.wait_ge(hot_ready[s], r + 1)
                pe.wait_ge(S["g_evac"], k + PRIMED)
                for n in range(8):
                    last = nc.tensor.matmul(gp[n // 2][:, n % 2 * 2 * P:(n % 2 + 1) * 2 * P], hot[s][:, n, 0, :],
                                            hot[s][:, n, 1:3, :].rearrange("p g k -> p (g k)"), start=True, stop=True)
                last.then_inc(g_full[s], 1)

            transposes(0, 0)
            with pe.Fori(0, N1) as r:
                for s in range(2):
                    step(s, r)
            with pe.Fori(N1, N1 + N2) as r:
                for s in range(2):
                    step(s, r)
            step(0, N1 + N2)
            pe.wait_ge(S["sel_ready"], NB * 2 + 1 + PRIMED)
            for n in range(3):
                if n == 2:
                    pe.wait_ge(S["selT_in"], 1)
                for b in range(NB):
                    last = nc.tensor.transpose(gp[n % 2][:, b * P:(b + 1) * P], sel[:, b, n, :], ident[:])
                last.then_inc(S["selT_full"], 1)
            with pe.Fori(0, N3 // 4) as q:
                for j in range(8):
                    step((j + 1) % 2, q * 4 + (N1 + N2 + (j + 1) // 2))
                    spread(j % 2, q * 4 + j // 2, q * 8 + j)
            step(1, N1 + N2 + N3)
            with pe.Fori(N1 + N2 + N3 + 1, KEYS // 2 - 1) as r:
                for s in range(2):
                    step(s, r)
            step(0, KEYS // 2 - 1)
            step(1, KEYS // 2 - 1, ahead=False)

        @block.scalar
        def _(act):
            def high(s, r):
                act.wait_ge(ut_full[s], r + 1 + PRIMED)
                act.wait_ge(u_mm[s], r + PRIMED)
                for g in range(2):
                    last = nc.scalar.activation(uh[s][:, 4 * g:4 * g + 4, :], utp[g][:], ACT.Copy)
                last.then_inc(ut_hi[s], 1)

            def gelu(s, r):
                act.wait_ge(u_mm[s], r + 1 + PRIMED)
                act.wait_ge(h_out[s], r * 16 + PRIMED * 16)
                nc.scalar.activation(hb[s][:], zb[s][:], ACT.Gelu).then_inc(h_done[s], 1)
                act.wait_ge(h_done[s], r + 1 + PRIMED)
                at = slice(r, r + 1) if isinstance(r, int) else ds(r, 1)
                act.dma_start(hv[:, at, s, :], hb[s][:].unsqueeze(1)).then_inc(h_out[s], 16)

            def step(s, r, ahead=True):
                if ahead:
                    high(1 - s, r + s)
                gelu(s, r)

            high(0, 0)
            with act.Fori(0, N1) as r:
                for s in range(2):
                    step(s, r)
            act.wait_ge(S["exp_in"], 1)
            nc.scalar.activation(sel[:, :, 2, :], sel[:, :, 2, :], ACT.Exp).then_inc(S["exp_out"], 1)
            nc.scalar.preload_act_table_set("gelu_and_others")
            with act.Fori(N1, N1 + N2) as r:
                for s in range(2):
                    step(s, r)
            step(0, N1 + N2)
            for n in range(2):
                act.wait_ge(S["selT_full"], n + 1)
                nc.scalar.activation(selT[:, n, :], gp[n][:], ACT.Copy).then_inc(S["selT_in"], 1)

            def evac(q, j):
                s = j % 2
                act.wait_ge(g_full[s], q * 4 + (j // 2 + 1) + PRIMED)
                act.wait_ge(g_sum[s], q * 4 + (j // 2 + PRIMED))
                for g in range(4):
                    last = nc.scalar.activation(parts[s][:, 2 * g:2 * g + 2].rearrange("p n g k -> p (n g k)"),
                                                gp[g][:], ACT.Copy)
                last.then_inc(S["g_evac"], 1)

            def send(q, half):
                for s in range(2):
                    act.wait_ge(g_sum[s], q * 4 + (2 * half + 2 + PRIMED))
                at = slice(q * 2 + half, q * 2 + half + 1) if isinstance(q, int) else ds(q * 2 + half, 1)
                act.dma_start(gd[:, :, :].rearrange("b p x -> p b x")[:, at, :],
                              grid[half][:].rearrange("p j n -> p (j n)").unsqueeze(1)).then_inc(g_out[half], 16)

            def tokens(q, steps):
                for j in steps:
                    step((j + 1) % 2, q * 4 + (N1 + N2 + (j + 1) // 2))
                    evac(q, j)
                    if j in (5, 9):
                        send(q, (j - 5) // 4)

            tokens(0, range(0, 2))
            with act.Fori(0, N3 // 4 - 1) as q:
                tokens(q, range(2, 10))
            tokens(N3 // 4 - 1, range(2, 8))
            step(1, N1 + N2 + N3)
            send(N3 // 4 - 1, 1)
            act.wait_ge(g_out[0], (N3 // 4 + PRIMED) * 16)
            down.rows_hi(act, 0, 0)
            with act.Fori(N1 + N2 + N3 + 1, KEYS // 2 - 1) as r:
                for s in range(2):
                    step(s, r)
            down.weights_hi(act, 0, 0)
            step(0, KEYS // 2 - 1)
            step(1, KEYS // 2 - 1, ahead=False)

        @block.gpsimd
        def _(pool):
            with pool.Fori(0, NB) as b:
                for n in range(2):
                    pool.wait_ge(eq_hot[n], b + 1)
                    view = eq[n][:].rearrange("p (h k) x -> p h k x", h=HEADS)
                    keys = picks_all[:, ds(b * HEADS, HEADS), 2 + n, :].unsqueeze(2)
                    nc.gpsimd.tensor_tensor(view, view, keys.broadcast_to([P, HEADS, TOPK, TOPK]),
                                            ALU.mult).then_inc(eq_key[n], 1)
            with pool.Fori(0, N3 // 4) as q:
                for j in range(8):
                    half, n0 = j // 4, j % 4 * 8
                    pool.wait_ge(S["g_evac"], q * 8 + (j + 1 + PRIMED))
                    if j % 4 == 0:
                        pool.wait_ge(g_out[half], q * 16 + PRIMED * 16)
                    nc.gpsimd.tensor_tensor(grid[half][:, :, n0:n0 + 8].rearrange("p k n -> p n k"), parts[j % 2][:, :, 0, :],
                                            parts[j % 2][:, :, 1, :], ALU.add).then_inc(g_sum[j % 2], 1)
            down.weights_lo(pool, 0, 0)

        @block.vector
        def _(dve):
            def low(s, r):
                dve.wait_ge(ut_hi[s], r + 1)
                for g in range(2):
                    last = nc.vector.tensor_tensor(ul[s][:, 4 * g:4 * g + 4, :].rearrange("p c f -> p (c f)"), utp[g][:],
                                                   uh[s][:, 4 * g:4 * g + 4, :].rearrange("p c f -> p (c f)").bitcast(F), ALU.subtract)
                last.then_inc(ut_lo[s], 1)

            def pick(u, k):
                v, done = nc.vector, S["pick"]
                best8, rest8 = slice(0, 8), slice(8, 16)
                flat = score[:].rearrange("p b (h q) k -> p (b h) q k", q=2)
                flat_c, flat_l = (t[:].rearrange("p u x y -> p u (x y)") for t in (cand, cleft))
                both = [(i, q) for i in range(2) for q in range(2)]
                if k == 0:
                    dve.drain()
                    dve.sem_clear(done)
                    v.tensor_copy(lists[:], flat[:, ds(u, 2), :, :]).then_inc(done, 1)
                elif k == 1:
                    dve.wait_ge(done, 1)
                    for i, q in both:
                        v.max(top[:, i, q, best8], lists[:, i, q, :]).then_inc(done, 1)
                elif k == 2:
                    dve.wait_ge(done, 5)
                    for i, q in both:
                        v.max_index(picks[:, i, 2 + q, best8], top[:, i, q, best8], lists[:, i, q, :]).then_inc(done, 1)
                elif k == 3:
                    for i, q in both:
                        v.match_replace(left[:, i, q, :], top[:, i, q, best8], lists[:, i, q, :], NEG).then_inc(done, 1)
                elif k == 4:
                    dve.wait_ge(done, 13)
                    for i, q in both:
                        v.max(top[:, i, q, rest8], left[:, i, q, :]).then_inc(done, 1)
                elif k == 5:
                    dve.wait_ge(done, 17)
                    for i, q in both:
                        v.max_index(picks[:, i, 2 + q, rest8], top[:, i, q, rest8], left[:, i, q, :]).then_inc(done, 1)
                elif k == 6:
                    v.tensor_tensor(cand[:], top[:, :, 0, :].unsqueeze(3).broadcast_to([P, 2, TOPK, TOPK]),
                                    top[:, :, 1, :].unsqueeze(2).broadcast_to([P, 2, TOPK, TOPK]), ALU.add).then_inc(done, 1)
                elif k == 7:
                    dve.wait_ge(done, 22)
                    for i in range(2):
                        v.max(best[:, i, best8], flat_c[:, i, :]).then_inc(done, 1)
                elif k == 8:
                    dve.wait_ge(done, 24)
                    for i in range(2):
                        v.match_replace(flat_l[:, i, :], best[:, i, best8], flat_c[:, i, :], NEG).then_inc(done, 1)
                elif k == 9:
                    for i in range(2):
                        v.max_index(pos[:, i, best8], best[:, i, best8], flat_c[:, i, :]).then_inc(done, 1)
                elif k == 10:
                    dve.wait_ge(done, 26)
                    for i in range(2):
                        v.max(best[:, i, rest8], flat_l[:, i, :]).then_inc(done, 1)
                elif k == 11:
                    dve.wait_ge(done, 30)
                    for i in range(2):
                        v.max_index(pos[:, i, rest8], best[:, i, rest8], flat_l[:, i, :]).then_inc(done, 1)
                elif k == 12:
                    dve.wait_ge(done, 32)
                    v.tensor_single_scalar(picks[:, :, 0, :], pos[:], 4, ALU.logical_shift_right).then_inc(done, 1)
                    v.tensor_single_scalar(picks[:, :, 1, :], pos[:], TOPK - 1, ALU.bitwise_and).then_inc(done, 1)
                    v.tensor_copy(best_all[:, ds(u, 2), :], best[:]).then_inc(S["picked"], 1)
                    dve.wait_ge(done, 34)
                    v.tensor_copy(picks_all[:, ds(u, 2), :, :], picks[:]).then_inc(S["picked"], 1)

            low(0, 0)
            STEPS = 13
            with dve.Fori(0, N1 // 5) as g:
                for j in range(10):
                    low(1 - j % 2, g * 5 + (j // 2 + j % 2))
                    for i in range(4 * STEPS * j // 10, 4 * STEPS * (j + 1) // 10):
                        pick(g * 8 + 2 * (i // STEPS), i % STEPS)
            dve.wait_ge(S["picked"], NB * HEADS)
            gates = sel[:, :, 2, :].rearrange("p b (h k) -> p b h k", h=HEADS)

            def per_head(t):
                return t.rearrange("p (b h) k -> p b h k", b=NB).broadcast_to([P, NB, HEADS, TOPK])

            nc.vector.tensor_tensor(gates, best_all[:].rearrange("p (b h) k -> p b h k", b=NB),
                                    per_head(best_all[:, :, 0:1]), ALU.subtract).then_inc(S["exp_in"], 1)

            def one_hots(b):
                dve.wait_ge(S["sel_ready"], b * 2 + PRIMED)
                for q in range(2):
                    place = picks_all[:, ds(b * HEADS, HEADS), q, :].unsqueeze(3)
                    nc.vector.tensor_tensor(
                        eq[q][:].rearrange("p (h k) x -> p h k x", h=HEADS),
                        place.broadcast_to([P, HEADS, TOPK, TOPK]),
                        iota[:, 0:TOPK].unsqueeze(1).unsqueeze(1).broadcast_to([P, HEADS, TOPK, TOPK]),
                        ALU.is_equal).then_inc(eq_hot[q], 1)

            def key(b, q):
                dve.wait_ge(eq_key[q], b + 1)
                nc.vector.tensor_reduce(sel[:, ds(b, 1), q, :], eq[q][:].unsqueeze(1), X, ALU.add).then_inc(S["sel_ready"], 1)

            with dve.Fori(0, NB // 2) as h:
                for i in range(2):
                    for j in range(3):
                        n = 3 * i + j
                        low(1 - n % 2, h * 3 + (N1 + n // 2 + n % 2))
                        if j == 0:
                            one_hots(h * 2 + i)
                        else:
                            key(h * 2 + i, j - 1)
            low(1, N1 + N2)
            dve.wait_ge(S["exp_out"], 1)
            nc.vector.tensor_reduce(total[:, 0, :].rearrange("p (b h) -> p b h", b=NB), gates, X,
                                    ALU.add).then_inc(S["gate_norm"], 1)
            dve.wait_ge(S["gate_norm"], 1)
            nc.vector.reciprocal(total[:, 1, :], total[:, 0, :]).then_inc(S["gate_norm"], 1)
            dve.wait_ge(S["gate_norm"], 2)
            nc.vector.tensor_tensor(gates, gates, per_head(total[:, 1, :].unsqueeze(2)), ALU.mult).then_inc(S["sel_ready"], 1)
            dve.wait_ge(S["selT_full"], 3)
            nc.vector.tensor_copy(gate_hi[:], gp[0][:]).then_inc(S["gate_split"], 1)
            dve.wait_ge(S["gate_split"], 1)
            nc.vector.tensor_tensor(gate_lo[:], gp[0][:], gate_hi[:].bitcast(F), ALU.subtract).then_inc(S["gate_split"], 1)
            dve.wait_ge(S["gate_split"], 2)
            dve.wait_ge(S["selT_in"], 2)
            with dve.Fori(0, N3 // 4) as q:
                for j in range(8):
                    s = j % 2
                    dve.wait_ge(g_full[s], q * 4 + j // 2 + PRIMED)
                    nc.vector.tensor_tensor(hot[s][:, :, 0, :], selT[:, 0, ds(q * 64 + 8 * j, 8)].unsqueeze(2).broadcast_to([P, 8, KEYS]),
                                            iota[:].unsqueeze(1).broadcast_to([P, 8, KEYS]), ALU.is_equal)
                    for n in range(8):
                        t = q * 64 + (8 * j + n)
                        for part, gate in ((1, gate_hi[:].bitcast(F)), (2, gate_lo[:])):
                            last = nc.vector.tensor_scalar(hot[s][:, n, part, :], iota[:], selT[:, 1, ds(t, 1)],
                                                           gate[:, ds(t, 1)], ALU.is_equal, ALU.mult)
                    last.then_inc(hot_ready[s], 1)
                    low(s, q * 4 + (N1 + N2 + 1 + j // 2))
            low(0, N1 + N2 + N3 + 1)
            with dve.Fori(N1 + N2 + N3 + 1, KEYS // 2 - 1) as r:
                for s in range(2):
                    low(1 - s, r + s)
            down.weights(dve, 0, 0)
            low(1, KEYS // 2 - 1)
            dve.wait_ge(g_out[1], (N3 // 4 + PRIMED) * 16)
            down.rows_lo(dve, 0, 0)
    return h_out


G4 = 4


class Stage:
    pass


def down_stage(nc, sem, m, a, hd, gd):
    d = Stage()
    d.raw = [m.put(f"v_raw{i}", 52 + 16 * i, [P, G4, D]) for i in range(2)]
    d.vh = [m.put(f"vh{i}", kb, [P, G4, D], R) for i, kb in enumerate((112, 84))]
    d.vl = [m.put(f"vl{i}", kb, [P, G4, D], R) for i, kb in enumerate((128, 16))]
    d.hb = [m.put(f"dh{i}", kb, [P, G4, T]) for i, kb in enumerate((199, 156))]
    d.gb = [m.put(f"dg{i}", 164 + 8 * i, [P, T // 32, G4, 32]) for i in range(2)]
    d.wh = [m.put(f"dwh{i}", kb, [P, G4, T], R) for i, kb in enumerate((180, 100))]
    d.wl = [m.put(f"dwl{i}", kb, [P, G4, T], R) for i, kb in enumerate((188, 32))]
    d.v_in, d.g_in, d.h_in, d.v_hi, d.v_lo, d.w_f, d.w_hi, d.w_lo = (
        [sem(f"d_{n}{i}") for i in range(2)] for n in ("v_in", "g_in", "h_in", "v_hi", "v_lo", "w_f", "w_hi", "w_lo"))
    vv = a["expert_v"][0].rearrange("(i r j) d -> i r (j d)", r=KEYS // G4, j=G4)
    hv = hd.rearrange("i (r j) t -> i r (j t)", j=G4)
    gv = gd.rearrange("b i (r x) -> i b r x", x=G4 * 32)

    def load_rows(eng, s, at):
        eng.dma_start(d.raw[s][:].rearrange("p j d -> p (j d)").unsqueeze(1), vv[:, at, :]).then_inc(d.v_in[s], 16)

    def load_acts(eng, s, at):
        eng.dma_start(d.hb[s][:].rearrange("p j t -> p (j t)").unsqueeze(1), hv[:, at, :]).then_inc(d.h_in[s], 16)

    def load_gates(eng, s, at):
        eng.dma_start(d.gb[s][:].rearrange("p b j n -> p b (j n)"),
                      gv[:, :, at, :].rearrange("p b o x -> p b (o x)")).then_inc(d.g_in[s], 16)

    def rows_hi(act, s, r):
        act.wait_ge(d.v_in[s], r * 16 + 16)
        nc.scalar.activation(d.vh[s][:], d.raw[s][:], ACT.Copy).then_inc(d.v_hi[s], 1)

    def rows_lo(dve, s, r):
        dve.wait_ge(d.v_hi[s], r + 1)
        nc.vector.tensor_tensor(d.vl[s][:], d.raw[s][:], d.vh[s][:].bitcast(F), ALU.subtract).then_inc(d.v_lo[s], 1)

    def weights(dve, s, r):
        dve.wait_ge(d.h_in[s], r * 16 + 16)
        dve.wait_ge(d.g_in[s], r * 16 + 16)
        w = d.hb[s][:].rearrange("p j (b n) -> p j b n", n=32)
        nc.vector.tensor_tensor(w, w, d.gb[s][:].rearrange("p b j n -> p j b n"), ALU.mult).then_inc(d.w_f[s], 1)

    def weights_hi(act, s, r):
        act.wait_ge(d.w_f[s], r + 1)
        nc.scalar.activation(d.wh[s][:], d.hb[s][:], ACT.Copy).then_inc(d.w_hi[s], 1)

    def weights_lo(pool, s, r):
        pool.wait_ge(d.w_hi[s], r + 1)
        nc.gpsimd.tensor_tensor(d.wl[s][:], d.hb[s][:], d.wh[s][:].bitcast(F), ALU.subtract).then_inc(d.w_lo[s], 1)

    d.load_rows, d.load_acts, d.load_gates, d.rows_hi, d.rows_lo = load_rows, load_acts, load_gates, rows_hi, rows_lo
    d.weights, d.weights_hi, d.weights_lo = weights, weights_hi, weights_lo
    return d


def down_program(nc, sem, psum, m, a, acc, d, h_out, out):
    ROUNDS = KEYS // G4 // 2
    fnorm = m.put("fnorm", 144, [P, D])
    fst = m.put("fst", 48, [P, 4, NB])
    ss, var, rs, tmp = (fst[:, i, :] for i in range(4))
    junk = m.put("junk", 148, [P, NB, D])

    o_full = [sem(f"d_o_full{i}") for i in range(2)]
    added = [sem(f"added{k}") for k in range(8)]
    S = {n: sem("d_" + n) for n in "fn_in sq root vchain normed out var".split()}

    with nc.Block() as block:
        @block.sync
        def _(sp_):
            for free in (*o_full, *added):
                sp_.sem_inc(free, PRIMED)
            sp_.dma_start(fnorm[:], a["final_norm"].unsqueeze(0).broadcast_to([P, D])).then_inc(S["fn_in"], 16)
            for s in range(2):
                sp_.wait_ge(h_out[s], (KEYS // 2 + PRIMED) * 16)
            with sp_.Fori(1, ROUNDS) as r:
                for s in range(2):
                    sp_.wait_ge(d.w_lo[s], r + PRIMED)
                    d.load_acts(sp_, s, ds(r * 2 + s, 1))
                    d.load_gates(sp_, s, ds(r * 2 + s, 1))
                    sp_.wait_ge(d.v_lo[s], r + PRIMED)
                    d.load_rows(sp_, s, ds(r * 2 + s, 1))
            for b in range(NB):
                sp_.wait_ge(S["normed"], b + 1)
                sp_.dma_start(out[0, b * P:(b + 1) * P, :], acc[:, b, :]).then_inc(S["out"], 16)
            sp_.wait_ge(S["out"], NB * 16)

        @block.scalar
        def _(act):
            d.rows_hi(act, 1, 0)
            d.weights_hi(act, 1, 0)
            with act.Fori(1, ROUNDS) as r:
                for s in range(2):
                    act.wait_ge(o_full[s], r * 8 + PRIMED)
                    d.rows_hi(act, s, r)
                    d.weights_hi(act, s, r)
            for b in range(NB):
                act.wait_ge(added[2 * b + 1], ROUNDS * 2 + PRIMED)
                nc.scalar.activation(junk[:, b, :], acc[:, b, :], ACT.Square, accum_out=ss[:, b:b + 1]).then_inc(S["sq"], 1)
                act.wait_ge(S["var"], b + 1)
                nc.scalar.activation(rs[:, b:b + 1], var[:, b:b + 1], ACT.Sqrt).then_inc(S["root"], 1)

        @block.gpsimd
        def _(pool):
            d.weights_lo(pool, 1, 0)
            with pool.Fori(1, ROUNDS) as r:
                for s in range(2):
                    d.weights_lo(pool, s, r)

        @block.tensor
        def _(pe):
            with pe.Fori(0, ROUNDS) as r:
                for s in range(2):
                    pe.wait_ge(d.v_lo[s], r + 1 + PRIMED)
                    pe.wait_ge(d.w_lo[s], r + 1 + PRIMED)
                    for k in range(8):
                        b, half = k // 2, k % 2
                        pe.wait_ge(added[k], r * 2 + s + PRIMED)
                        for j in range(G4):
                            for n, (w, v) in enumerate(((d.wh, d.vh), (d.wh, d.vl), (d.wl, d.vh))):
                                last = nc.tensor.matmul(psum[k][:], w[s][:, j, b * P:(b + 1) * P],
                                                        v[s][:, j, half * T:(half + 1) * T],
                                                        start=(j == 0 and n == 0), stop=(j == G4 - 1 and n == 2))
                        last.then_inc(o_full[s], 1)

        @block.vector
        def _(dve):
            def prepare(s, r):
                d.weights(dve, s, r)
                d.rows_lo(dve, s, r)

            def add(s, r, after=None):
                for k in range(8):
                    if after is not None and k % 2 == 0 and k:
                        after(k // 2 - 1)
                    b, half = k // 2, k % 2
                    dve.wait_ge(o_full[s], r * 8 + (k + 1) + PRIMED)
                    part = acc[:, b, half * T:(half + 1) * T]
                    nc.vector.tensor_tensor(part, part, psum[k][:], ALU.add).then_inc(added[k], 1)

            with dve.Fori(0, ROUNDS - 1) as r:
                prepare(1, r)
                add(0, r)
                prepare(0, r + 1)
                add(1, r)
            prepare(1, ROUNDS - 1)
            add(0, ROUNDS - 1)
            done = [0]

            def chain(ins):
                done[0] += 1
                ins.then_inc(S["vchain"], 1)
                dve.wait_ge(S["vchain"], done[0])

            def norm_out(b):
                va, r, t = (x[:, b:b + 1] for x in (var, rs, tmp))
                dve.wait_ge(S["sq"], b + 1)
                nc.vector.tensor_scalar(va, ss[:, b:b + 1], 1.0 / D, EPS, ALU.mult, ALU.add).then_inc(S["var"], 1)
                dve.wait_ge(S["root"], b + 1)
                chain(nc.vector.reciprocal(r, r))
                chain(nc.vector.tensor_tensor(t, r, r, ALU.mult))
                chain(nc.vector.tensor_tensor(t, t, va, ALU.mult))
                chain(nc.vector.tensor_scalar(t, t, -0.5, 1.5, ALU.mult, ALU.add))
                chain(nc.vector.tensor_tensor(r, r, t, ALU.mult))
                nc.vector.scalar_tensor_tensor(acc[:, b, :], acc[:, b, :], r, fnorm[:], ALU.mult,
                                               ALU.mult).then_inc(S["normed"], 1)

            dve.wait_ge(S["fn_in"], 16)
            add(1, ROUNDS - 1, after=norm_out)
            norm_out(NB - 1)


def layer(nc, a, out):
    ctx = ExitStack()
    with ctx:
        def sem(name):
            return ctx.enter_context(nc.semaphore(name))

        psum = [ctx.enter_context(nc.psum_tensor(f"bank{i}", [P, T], F)) for i in range(8)]
        m = Map(nc, (nc.sbuf_base + 63) // 64 * 64)
        acc = m.put("acc", 0, [P, NB, D])
        sT = m.put("xTh", 16, [P, C, T], R), m.put("xTl", 32, [P, C, T], R)
        const = {n: m.put(n, 48 + i / 2, [P, P])
                 for i, n in enumerate(("ident", "iota", "tri", "ones", "causal", "gap"))}
        const["vecs"] = m.put("vecs", 51, [P, 32])
        hd = nc.dram_tensor("expert_act", (P, KEYS, T), F).ap()
        gd = nc.dram_tensor("expert_gate", (T // 32, P, KEYS * 32), F).ap()
        u_raw = [m.put(f"u_raw{i}", 100 + 4 * i, [P, D]) for i in range(2)]
        u_in = [sem(f"u_in{i}") for i in range(2)]
        u_view = a["expert_u"][0].rearrange("(i j) d -> i j d", j=KEYS)
        score = mix_program(nc, sem, psum, m, a, acc, sT, const, u_raw, u_in, u_view)
        down = down_stage(nc, sem, m, a, hd, gd)
        h_out = up_program(nc, sem, psum, m, sT, const, score, hd, gd, u_raw, u_in, u_view, down)
        down_program(nc, sem, psum, m, a, acc, down, h_out, out)


_INS = ["x", "norm_mix", "w_in", "conv_w", "conv_b", "w_branch_a", "w_branch_b", "w_out", "norm_ffn", "w_q",
        "sub_keys", "expert_u", "expert_v", "final_norm"]


def kernel(**inputs):
    import concourse.bacc as _bacc
    from concourse.bass_utils import run_bass_kernel_spmd as _run

    nc = _bacc.Bacc("TRN2", target_bir_lowering=False, num_devices=1)
    arrays, a = {}, {}
    for name in _INS:
        x = np.ascontiguousarray(inputs[name])
        arrays[f"in_{name}"] = x
        a[name] = nc.dram_tensor(f"in_{name}", x.shape, mybir.dt.from_np(x.dtype), kind="ExternalInput").ap()
    out = nc.dram_tensor("out_0", (1, T, D), F, kind="ExternalOutput").ap()
    layer(nc, a, out)
    r = _run(nc, [arrays], core_ids=[0])
    return r.results[0]["out_0"]
```
